# Optimizing a Trainium2 kernel written in Bass

```python
import jax, jax.numpy as jnp
from jax import lax
import numpy as np

D_MODEL = 1024
BATCH = 1
SEQ = 2048
DEPTH = 1
DEC_BATCH = 1
DEC_SEQ = 32
PAST_LEN = 4096

CHUNK = 64
Q_BLOCK = 128
FOX_HEADS = 8
FOX_HEAD_DIM = 64
FOX_WIDTH = FOX_HEADS * FOX_HEAD_DIM
GLA_HEADS = 4
GLA_DK = 64
GLA_DV = 128
GLA_KW = GLA_HEADS * GLA_DK
GLA_VW = GLA_HEADS * GLA_DV
GLA_GATE_RANK = 16
GLA_GATE_TEMP = 16.0
MIX_WIDTH = FOX_WIDTH + GLA_VW
D_FF = -(-8 * D_MODEL // (3 * 256)) * 256
EPS = 1e-6

SPLIT_SIZES = (FOX_WIDTH, FOX_WIDTH, FOX_WIDTH, FOX_HEADS,
               GLA_KW, GLA_KW, GLA_VW, GLA_GATE_RANK, GLA_VW)
SPLIT_IDX = tuple(int(s) for s in np.cumsum(SPLIT_SIZES)[:-1])
IN_WIDTH = int(sum(SPLIT_SIZES))

kernel_name = 'fox_gla_parallel_heads_stream_step'

def _rmsnorm(x, g):
    xf = x.astype(jnp.float32)
    y = xf * lax.rsqrt(jnp.mean(jnp.square(xf), axis=-1, keepdims=True) + EPS)
    return (y * g.astype(jnp.float32)).astype(x.dtype)

def _project(h, w_in, w_gate2, b_gate2, b_forget):
    B, T, _ = h.shape
    z = h @ w_in
    fq, fk, fv, fl, gq, gk, gv, gg, gr = jnp.split(z, SPLIT_IDX, axis=-1)
    heads = lambda a, n, d: a.reshape(B, T, n, d)
    logf = jax.nn.log_sigmoid((fl + b_forget).astype(jnp.float32))
    glog = jax.nn.log_sigmoid((gg @ w_gate2 + b_gate2).astype(jnp.float32)) / GLA_GATE_TEMP
    return (heads(fq, FOX_HEADS, FOX_HEAD_DIM), heads(fk, FOX_HEADS, FOX_HEAD_DIM),
            heads(fv, FOX_HEADS, FOX_HEAD_DIM), logf,
            heads(gq, GLA_HEADS, GLA_DK), heads(gk, GLA_HEADS, GLA_DK),
            heads(gv, GLA_HEADS, GLA_DV), heads(glog, GLA_HEADS, GLA_DK), gr)

def _fox_prompt(q, k, v, logf):
    B, T, H, D = q.shape
    scale = D ** -0.5
    c = jnp.cumsum(logf, axis=1).transpose(0, 2, 1)
    n_blocks = T // Q_BLOCK
    q_blocks = q.reshape(B, n_blocks, Q_BLOCK, H, D).swapaxes(0, 1)
    c_blocks = c.reshape(B, H, n_blocks, Q_BLOCK).transpose(2, 0, 1, 3)
    key_pos = jnp.arange(T)

    def one_block(args):
        blk, qb, cb = args
        s = jnp.einsum('bqhd,bkhd->bhqk', qb, k).astype(jnp.float32) * scale
        s = s + cb[..., None] - c[:, :, None, :]
        q_pos = blk * Q_BLOCK + jnp.arange(Q_BLOCK)
        s = jnp.where(key_pos[None, :] <= q_pos[:, None], s, -jnp.inf)
        p = jax.nn.softmax(s, axis=-1).astype(v.dtype)
        return jnp.einsum('bhqk,bkhd->bqhd', p, v)

    o = lax.map(one_block, (jnp.arange(n_blocks), q_blocks, c_blocks))
    return o.swapaxes(0, 1).reshape(B, T, H * D)

def _fox_sample(q, k, v, logf, ck, cv, clogf):
    B, T, H, D = q.shape
    P = ck.shape[1]
    scale = D ** -0.5
    clogf = clogf.astype(jnp.float32)
    c_new = jnp.cumsum(logf, axis=1).transpose(0, 2, 1)
    suffix = (jnp.cumsum(clogf[:, ::-1], axis=1)[:, ::-1] - clogf).transpose(0, 2, 1)
    s_past = (jnp.einsum('bqhd,bkhd->bhqk', q, ck).astype(jnp.float32) * scale
              + c_new[..., None] + suffix[:, :, None, :])
    s_new = (jnp.einsum('bqhd,bkhd->bhqk', q, k).astype(jnp.float32) * scale
             + c_new[..., None] - c_new[:, :, None, :])
    s_new = jnp.where(jnp.tril(jnp.ones((T, T), bool)), s_new, -jnp.inf)
    p = jax.nn.softmax(jnp.concatenate([s_past, s_new], axis=-1), axis=-1).astype(v.dtype)
    o = (jnp.einsum('bhqk,bkhd->bqhd', p[..., :P], cv)
         + jnp.einsum('bhqk,bkhd->bqhd', p[..., P:], v))
    return o.reshape(B, T, H * D)

def _gla_chunk(S, inp):
    q, k, v, g = inp
    L = q.shape[1]
    qf = q.astype(jnp.float32) * (GLA_DK ** -0.5)
    kf = k.astype(jnp.float32)
    vf = v.astype(jnp.float32)
    b = jnp.cumsum(g, axis=1)
    o_inter = jnp.einsum('blhk,bhkv->blhv', qf * jnp.exp(b), S)
    tri = jnp.tril(jnp.ones((L, L), bool))[None, :, :, None, None]
    diff = b[:, :, None] - b[:, None, :]
    decay = jnp.exp(jnp.where(tri, diff, -jnp.inf))
    A = jnp.einsum('bthk,bshk,btshk->bhts', qf, kf, decay)
    o_intra = jnp.einsum('bhts,bshv->bthv', A, vf)
    b_last = b[:, -1]
    k_dec = kf * jnp.exp(b_last[:, None] - b)
    S_new = jnp.exp(b_last)[..., None] * S + jnp.einsum('blhk,blhv->bhkv', k_dec, vf)
    return S_new, o_inter + o_intra

def _gla_prompt(q, k, v, g):
    B, T = q.shape[:2]
    n = T // CHUNK
    to_chunks = lambda a: a.reshape(B, n, CHUNK, *a.shape[2:]).swapaxes(0, 1)
    S0 = jnp.zeros((B, GLA_HEADS, GLA_DK, GLA_DV), jnp.float32)
    S, o = lax.scan(_gla_chunk, S0, (to_chunks(q), to_chunks(k), to_chunks(v), to_chunks(g)))
    return o.swapaxes(0, 1).reshape(B, T, GLA_HEADS, GLA_DV), S

def _merge(fox_o, gla_o, gr, gla_norm_g, w_out):
    B, T = fox_o.shape[:2]
    gn = gla_o * lax.rsqrt(jnp.mean(jnp.square(gla_o), axis=-1, keepdims=True) + EPS)
    gated = gn.reshape(B, T, GLA_VW) * gla_norm_g.astype(jnp.float32) * jax.nn.silu(gr.astype(jnp.float32))
    mix = jnp.concatenate([fox_o, gated.astype(fox_o.dtype)], axis=-1)
    return mix @ w_out

def _swiglu(h, w_gate, w_up, w_down):
    return (jax.nn.silu(h @ w_gate) * (h @ w_up)) @ w_down

def setup_inputs(seed: int = 0) -> dict:
    key = jax.random.key(seed)
    ks = jax.random.split(key, 20)
    nrm = lambda k, shape, s=1.0: s * jax.random.normal(k, shape, jnp.float32)
    return {
        'x_prompt': nrm(ks[0], (BATCH, SEQ, D_MODEL)),
        'x_sample': nrm(ks[1], (DEC_BATCH, DEC_SEQ, D_MODEL)),
        'cache_fox_k': nrm(ks[2], (DEPTH, DEC_BATCH, PAST_LEN, FOX_HEADS, FOX_HEAD_DIM)),
        'cache_fox_v': nrm(ks[3], (DEPTH, DEC_BATCH, PAST_LEN, FOX_HEADS, FOX_HEAD_DIM)),
        'cache_fox_logf': jax.nn.log_sigmoid(1.0 + nrm(ks[4], (DEPTH, DEC_BATCH, PAST_LEN, FOX_HEADS))),
        'state_gla': nrm(ks[5], (DEPTH, DEC_BATCH, GLA_HEADS, GLA_DK, GLA_DV), 0.5),
        'norm1_g': 1.0 + nrm(ks[6], (DEPTH, D_MODEL), 0.02),
        'w_in': nrm(ks[7], (DEPTH, D_MODEL, IN_WIDTH), D_MODEL ** -0.5),
        'w_gate2': nrm(ks[8], (DEPTH, GLA_GATE_RANK, GLA_KW), GLA_GATE_RANK ** -0.5),
        'b_gate2': nrm(ks[9], (DEPTH, GLA_KW), 0.1),
        'b_forget': 1.0 + nrm(ks[10], (DEPTH, FOX_HEADS), 0.5),
        'gla_norm_g': 1.0 + nrm(ks[11], (DEPTH, GLA_VW), 0.02),
        'w_out': nrm(ks[12], (DEPTH, MIX_WIDTH, D_MODEL), MIX_WIDTH ** -0.5),
        'norm2_g': 1.0 + nrm(ks[13], (DEPTH, D_MODEL), 0.02),
        'w_gate': nrm(ks[14], (DEPTH, D_MODEL, D_FF), D_MODEL ** -0.5),
        'w_up': nrm(ks[15], (DEPTH, D_MODEL, D_FF), D_MODEL ** -0.5),
        'w_down': nrm(ks[16], (DEPTH, D_FF, D_MODEL), D_FF ** -0.5),
        'final_norm_g': 1.0 + nrm(ks[17], (D_MODEL,), 0.02),
    }

def reference(x_prompt, x_sample, cache_fox_k, cache_fox_v, cache_fox_logf, state_gla,
              norm1_g, w_in, w_gate2, b_gate2, b_forget, gla_norm_g, w_out,
              norm2_g, w_gate, w_up, w_down, final_norm_g):
    y_p, y_s = x_prompt, x_sample
    k_p, v_p, lf_p, s_p = [], [], [], []
    k_s, v_s, lf_s, s_s = [], [], [], []
    for layer in range(DEPTH):
        h = _rmsnorm(y_p, norm1_g[layer])
        fq, fk, fv, logf, gq, gk, gv, glog, gr = _project(h, w_in[layer], w_gate2[layer],
                                                          b_gate2[layer], b_forget[layer])
        fox_o = _fox_prompt(fq, fk, fv, logf)
        gla_o, S = _gla_prompt(gq, gk, gv, glog)
        y_p = y_p + _merge(fox_o, gla_o, gr, gla_norm_g[layer], w_out[layer])
        y_p = y_p + _swiglu(_rmsnorm(y_p, norm2_g[layer]), w_gate[layer], w_up[layer], w_down[layer])
        k_p.append(fk); v_p.append(fv); lf_p.append(logf); s_p.append(S)

        h = _rmsnorm(y_s, norm1_g[layer])
        fq, fk, fv, logf, gq, gk, gv, glog, gr = _project(h, w_in[layer], w_gate2[layer],
                                                          b_gate2[layer], b_forget[layer])
        fox_o = _fox_sample(fq, fk, fv, logf, cache_fox_k[layer], cache_fox_v[layer],
                            cache_fox_logf[layer])
        S, gla_o = _gla_chunk(state_gla[layer].astype(jnp.float32), (gq, gk, gv, glog))
        y_s = y_s + _merge(fox_o, gla_o, gr, gla_norm_g[layer], w_out[layer])
        y_s = y_s + _swiglu(_rmsnorm(y_s, norm2_g[layer]), w_gate[layer], w_up[layer], w_down[layer])
        k_s.append(fk); v_s.append(fv); lf_s.append(logf); s_s.append(S)

    y_prompt = _rmsnorm(y_p, final_norm_g)
    y_sample = _rmsnorm(y_s, final_norm_g)
    return (y_prompt, y_sample,
            jnp.stack(k_p), jnp.stack(v_p), jnp.stack(lf_p), jnp.stack(s_p),
            jnp.stack(k_s), jnp.stack(v_s), jnp.stack(lf_s), jnp.stack(s_s))


_drawn_inputs = setup_inputs


def setup_inputs(seed=0):
    import zlib

    import numpy as np

    out = dict(_drawn_inputs(seed))
    spreads = {}
    factors = {'gla_norm_g': 6.518, 'norm2_g': 4.122, 'final_norm_g': 2.875}
    for name, (base, spread) in spreads.items():
        noise = np.random.default_rng([zlib.crc32(name.encode()), seed]).standard_normal(out[name].shape)
        drawn = base * np.exp(spread * noise) if base else spread * noise
        out[name] = __import__('jax').numpy.asarray(drawn.astype(out[name].dtype))
    for name, factor in factors.items():
        out[name] = (out[name] * factor).astype(out[name].dtype)
    return out
```

```python
from contextlib import ExitStack

import numpy as np
import concourse.bass as bass
from concourse import mybir

F32 = mybir.dt.float32
F32R = mybir.dt.float32r
BF16 = mybir.dt.bfloat16
U32 = mybir.dt.uint32
ALU = mybir.AluOpType
ACT = mybir.ActivationFunctionType
AX = mybir.AxisListType

P = 128
D = 1024
KD = D // P
SEQ = 2048
NEW = 32
NTOK = SEQ + NEW
PAST = 4096
TT = 104
NT = NTOK // TT
LAST_PROMPT = SEQ - (NT - 1) * TT
HEADS = 8
HD = 64
FOX = HEADS * HD
GH = 4
GK = 64
GV = 128
GKW = GH * GK
GVW = GH * GV
RANK = 16
TEMP = 16.0
DFF = 2816
EPS = 1e-6
C_Q, C_K, C_V, C_F = 0, FOX, 2 * FOX, 3 * FOX
C_GQ = C_F + HEADS
C_GK = C_GQ + GKW
C_GV = C_GK + GKW
C_GG = C_GV + GVW
C_GR = C_GG + RANK
IN_WIDTH = C_GR + GVW
SCALE = HD ** -0.5
HI, LO = 0, 1
PASSES = ((HI, HI), (HI, LO), (LO, HI))


def scope(nc, ctx):
    sems = []

    def retire():
        nc.clear_and_free_semaphores(sems)
        nc.all_engine_barrier()
    ctx.callback(retire)

    def sb(name, shape, dt=F32):
        return ctx.enter_context(nc.sbuf_tensor(name, shape, dt))

    def sem(name):
        sems.append(nc.alloc_semaphore(name))
        return sems[-1]

    def psum(name):
        return ctx.enter_context(nc.psum_tensor(name, [P, 8, 512], F32))
    return sb, sem, psum


def skewed(e, n, front, back, m=2):
    front(0, 0)
    with e.Fori(0, n // m - 1) as i:
        for j in range(m):
            front(m * i + j + 1, (j + 1) % m)
            back(m * i + j, j)
    for j in range(m):
        if j < m - 1:
            front(n - m + j + 1, j + 1)
        back(n - m + j, j)


def paired(e, n, tile):
    with e.Fori(0, n // 2) as i:
        tile(2 * i, 0)
        tile(2 * i + 1, 1)


def fill_identity(pool, ident, filled):
    pool.memset(ident[:], 0.0).then_inc(filled, 1)
    pool.wait_ge(filled, 1)
    pool.affine_select(out=ident[:], in_=ident[:], compare_op=ALU.not_equal, fill=1.0, base=0,
                       pattern=[[-1, P]], channel_multiplier=1).then_inc(filled, 1)


TCOLS = [C_Q + P * n for n in range(4)] + [C_GQ + P * n for n in range(4)]
RCOLS = ([C_K + P * n for n in range(4)] + [C_V + P * n for n in range(4)]
         + [C_GV + P * n for n in range(4)] + [C_GR + P * n for n in range(4)])
NTT, NTR = len(TCOLS), len(RCOLS)
NWT = NTT + NTR + 1
R_Q, R_GQ, R_GK, R_K, R_F, R_GG = 0, 512, 768, 1024, 1536, 1544
XB = 4
NB = 5
BLK = NTOK // NB
TPB = BLK // TT


def project(nc, d):
    with ExitStack() as ctx:
        sb, sem, psum = scope(nc, ctx)
        hT = sb("hT", [P, NT, 2, KD, TT], F32R)
        ident = sb("ident", [P, P])
        grow = sb("grow", [TT, D])
        xn = sb("xn", [TT, 2, D])
        msq = sb("msq", [TT, 2])
        rms = sb("rms", [TT, 2])
        inv = sb("inv", [TT, 2])
        eps = sb("eps", [P, 1])
        wraw = sb("wraw", [P, 2, KD, P])
        wsp = sb("wsp", [P, 2, 2, KD, P], F32R)
        zs = sb("zs", [P, 2, NTOK])
        xin = zs[0:TT].rearrange("p a t -> p (a t)")[:, 0:XB * D].rearrange("p (b c) -> p b c", b=XB)
        zr = sb("zr", [TT, NT, P])
        ps = psum("ps_project")
        x_in = [sem(f"x_in{b}") for b in range(XB)]
        g_in, filled, eps_set = sem("g_in"), sem("filled"), sem("eps_set")
        squared, rooted, inverted = sem("squared"), sem("rooted"), sem("inverted")
        x_scaled, x_turned, h_hi, h_lo = sem("x_scaled"), sem("x_turned"), sem("h_hi"), sem("h_lo")
        w_come = [sem("w_come0"), sem("w_come1")]
        w_hi, w_lo = sem("w_hi"), sem("w_lo")
        block_done, block_out = sem("block_done"), sem("block_out")
        rows_turned, rows_out = sem("rows_turned"), sem("rows_out")
        t_stored = [sem("t_stored0"), sem("t_stored1")]
        r_stored = sem("r_stored")
        block = ctx.enter_context(nc.Block())
        X_CREDIT = 2
        B_CREDIT = 2 * NB
        R_CREDIT = 2

        @block.sync
        def _(sp):
            for b in range(2):
                sp.sem_inc(t_stored[b], 16)
            sp.sem_inc(r_stored, 48)
            w = d["w_in"][0].rearrange("(k p) n -> p k n", p=P)

            def load_w(n):
                b = n % 2
                if n >= 2:
                    sp.wait_ge(w_lo, n - 1)
                if n < NTT + NTR:
                    c = (TCOLS + RCOLS)[n]
                    sp.dma_start(wraw[:, b], w[:, :, c:c + P]).then_inc(w_come[b], 16)
                else:
                    sp.dma_start(wraw[:, b, :, 0:HEADS], w[:, :, C_F:C_F + HEADS]).then_inc(w_come[b], 16)
                    sp.dma_start(wraw[:, b, :, HEADS:HEADS + RANK], w[:, :, C_GG:C_GR]).then_inc(w_come[b], 16)

            def load_x(t, b):
                sp.wait_ge(x_scaled, t + 1)
                sp.dma_start(xin[:, b], d["x_prompt"][0, bass.ds(t * TT, TT), :]).then_inc(x_in[b], 16)

            sp.dma_start(grow[:], d["norm1_g"].partition_broadcast(TT)).then_inc(g_in, 16)
            with sp.Fori(0, NT // XB - 1) as i:
                for b in range(XB):
                    load_x(XB * i + b, b)
            load_w(0)
            load_w(1)
            for b in range(XB - 1):
                load_x(NT - XB + b, b)
            sp.wait_ge(x_scaled, NT)
            sp.dma_start(xin[0:LAST_PROMPT, XB - 1], d["x_prompt"][0, (NT - 1) * TT:SEQ, :]).then_inc(x_in[XB - 1], 16)
            sp.dma_start(xin[LAST_PROMPT:TT, XB - 1], d["x_sample"][0]).then_inc(x_in[XB - 1], 16)

            def store_t(n, row, rows):
                sp.wait_ge(block_out, NB * (n + 1) + B_CREDIT)
                sp.dma_start(d["zT"][row:row + rows, :], zs[0:rows, n % 2]).then_inc(t_stored[n % 2], 16)

            def store_rows(n, prompt, sample, c):
                sp.wait_ge(rows_out, NB * (n - NTT + 1) + R_CREDIT)
                full = (NT - 1) * TT
                sp.dma_start(prompt[0:full, c:c + P].rearrange("(t p) c -> p t c", p=TT),
                             zr[:, 0:NT - 1, :]).then_inc(r_stored, 16)
                sp.dma_start(prompt[full:SEQ, c:c + P], zr[0:LAST_PROMPT, NT - 1, :]).then_inc(r_stored, 16)
                sp.dma_start(sample[:, c:c + P], zr[LAST_PROMPT:TT, NT - 1, :]).then_inc(r_stored, 16)

            t_rows = [R_Q + P * j for j in range(4)] + [R_GQ + P * j for j in range(4)] + [R_K + P * j for j in range(4)]
            row_outs = [(d["new_k_p"], d["new_k_s"]), (d["new_v_p"], d["new_v_s"]),
                        (d["zrow"][0:SEQ, 0:GVW], d["zrow"][SEQ:NTOK, 0:GVW]),
                        (d["zrow"][0:SEQ, GVW:2 * GVW], d["zrow"][SEQ:NTOK, GVW:2 * GVW])]
            for n in range(NWT):
                if 1 <= n < NWT - 1:
                    load_w(n + 1)
                if n < len(t_rows):
                    store_t(n, t_rows[n], P)
                elif n == NWT - 1:
                    store_t(n, R_F, HEADS + RANK)
                if NTT <= n < NTT + NTR:
                    j = n - NTT
                    store_rows(n, *row_outs[j // 4], P * (j % 4))
            for b in range(2):
                sp.wait_ge(t_stored[b], 16 * (1 + len(t_rows) // 2 + (b == 0)))
            sp.wait_ge(r_stored, 48 * (NTR + 1))

        @block.gpsimd
        def _(pool):
            pool.memset(eps[:], EPS).then_inc(eps_set, 1)
            fill_identity(pool, ident, filled)

        def tile_loops(e, front, back_t, back_k, back_r):
            front(0, 0)
            for lo, hi, back in ((0, NTT, back_t), (NTT, NTT + 4, back_k), (NTT + 4, NTT + NTR, back_r)):
                rounds = (hi - lo) // 2 - (hi == NWT - 1)
                with e.Fori(0, rounds) as i:
                    front(lo + 2 * i + 1, 1)
                    back(lo + 2 * i, 0)
                    front(lo + 2 * i + 2, 0)
                    back(lo + 2 * i + 1, 1)
            front(hi - 1, 1)
            back(hi - 2, 0)
            front(hi, 0, True)
            back(hi - 1, 1)
            back_t(hi, 0)

        def come(n, b, last):
            return 8 * (n - b) + (32 if last else 16)

        @block.scalar
        def _(act):
            act.sem_inc(block_out, B_CREDIT)
            act.wait_ge(eps_set, 1)

            def square(t, q):
                b = q % 2
                act.wait_ge(x_in[q], 16 // XB * (t - q) + (16 if not isinstance(t, int) or t < NT - 1 else 32))
                act.activation(ps[0:TT, 4 + 2 * b:6 + 2 * b, :].rearrange("p a c -> p (a c)"), xin[:, q], ACT.Square,
                               accum_out=msq[:, b:b + 1]).then_inc(squared, 1)
                act.wait_ge(squared, t + 1)
                act.wait_ge(inverted, t - 1 + X_CREDIT)
                act.activation(rms[:, b:b + 1], msq[:, b:b + 1], ACT.Sqrt, scale=1.0 / D, bias=eps[0:TT]).then_inc(rooted, 1)

            def hi_h(t, q):
                b = q % 2
                act.wait_ge(x_turned, t + 1 + X_CREDIT)
                act.activation(hT[:, bass.ds(t, 1), HI].rearrange("p o (a k) t -> p (o a) (k t)", a=2),
                               ps[:, 2 * b:2 * b + 2, 0:4 * TT], ACT.Copy).then_inc(h_hi, 1)

            skewed(act, NT, square, hi_h, XB)

            def hi_w(n, b, last=False):
                act.wait_ge(w_come[b], come(n, b, last))
                act.wait_ge(block_done, NB * (n - 1) + B_CREDIT)
                act.activation(wsp[:, b, HI], wraw[:, b], ACT.Copy).then_inc(w_hi, 1)

            def out_blocks(n, b, stored):
                act.wait_ge(t_stored[b], stored)
                for g in range(NB):
                    act.wait_ge(block_done, NB * n + g + 1 + B_CREDIT)
                    act.activation(zs[:, b, g * BLK:(g + 1) * BLK], ps[:, g, 0:BLK], ACT.Copy).then_inc(block_out, 1)

            tile_loops(act, hi_w, lambda n, b: out_blocks(n, b, 8 * (n - b) + 16 if not isinstance(n, int) else 16 * (NTT // 2 + 3)),
                       lambda n, b: out_blocks(n, b, 8 * (n - b) + 16),
                       lambda n, b: out_blocks(n, b, 16 * ((NTT + 4) // 2 + 1)))

        @block.vector
        def _(dve):
            dve.sem_inc(x_scaled, XB)
            dve.sem_inc(inverted, X_CREDIT)
            dve.sem_inc(h_lo, X_CREDIT)
            dve.sem_inc(rows_out, R_CREDIT)
            dve.wait_ge(g_in, 16)

            def scale_x(t, q):
                b = q % 2
                dve.wait_ge(rooted, t + 1)
                dve.reciprocal(inv[:, b:b + 1], rms[:, b:b + 1]).then_inc(inverted, 1)
                dve.wait_ge(inverted, t + 1 + X_CREDIT)
                dve.wait_ge(x_turned, t - 1 + X_CREDIT)
                dve.scalar_tensor_tensor(out=xn[:, b], in0=xin[:, q], scalar=inv[:, b:b + 1], in1=grow[:],
                                         op0=ALU.mult, op1=ALU.mult).then_inc(x_scaled, 1)

            def lo_h(t, q):
                b = q % 2
                dve.wait_ge(h_hi, t + 1)
                part = lambda s: hT[:, bass.ds(t, 1), s].rearrange("p o (a k) t -> p (o a) (k t)", a=2)
                dve.tensor_tensor(part(LO), ps[:, 2 * b:2 * b + 2, 0:4 * TT], part(HI).bitcast(F32),
                                  ALU.subtract).then_inc(h_lo, 1)

            skewed(dve, NT, scale_x, lo_h, XB)

            def lo_w(n, b, last=False):
                dve.wait_ge(w_hi, n + 1)
                dve.tensor_tensor(wsp[:, b, LO], wraw[:, b], wsp[:, b, HI].bitcast(F32), ALU.subtract).then_inc(w_lo, 1)

            def out_rows(n, b):
                r = n - NTT
                dve.wait_ge(r_stored, 48 * r + 48)
                for g in range(NB):
                    dve.wait_ge(rows_turned, NB * r + g + 1)
                    dve.tensor_copy(zr[:, g * TPB:(g + 1) * TPB, :],
                                    ps[0:TT, 5 + (b * NB + g) % 2, :].rearrange("p (t c) -> p t c", c=P)).then_inc(rows_out, 1)

            tile_loops(dve, lo_w, lambda n, b: None, out_rows, out_rows)

        @block.tensor
        def _(pe):
            pe.sem_inc(x_turned, X_CREDIT)
            pe.sem_inc(block_done, B_CREDIT)
            pe.wait_ge(filled, 2)

            def turn_x(t, b):
                pe.wait_ge(x_scaled, t + 1 + XB)
                pe.wait_ge(h_lo, t - 1 + X_CREDIT)
                for k in range(KD):
                    last = pe.transpose(ps[:, 2 * b + k // 4, (k % 4) * TT:(k % 4 + 1) * TT],
                                        xn[:, b, k * P:(k + 1) * P], ident[0:TT, 0:TT])
                last.then_inc(x_turned, 1)

            paired(pe, NT, turn_x)
            pe.wait_ge(h_lo, NT + X_CREDIT)

            def products(n, b, g):
                pe.wait_ge(block_out, NB * (n - 1) + g + 1 + B_CREDIT)
                m = 0
                for k in range(KD):
                    for s, v in PASSES:
                        last = pe.matmul(ps[:, g, 0:BLK], wsp[:, b, s, k, :], hT[:, g * TPB:(g + 1) * TPB, v, k, :],
                                         start=m == 0, stop=m == 3 * KD - 1)
                        m += 1
                last.then_inc(block_done, 1)

            def turn_rows(n, b, g):
                r = n - NTT
                pe.wait_ge(block_out, NB * n + g + 1 + B_CREDIT)
                pe.wait_ge(rows_out, NB * r + g - 1 + R_CREDIT)
                for q in range(TPB):
                    t = g * TPB + q
                    last = pe.transpose(ps[0:TT, 5 + (b * NB + g) % 2, q * P:(q + 1) * P],
                                        zs[:, b, t * TT:(t + 1) * TT], ident[:])
                last.then_inc(rows_turned, 1)

            def tile_t(n, b):
                pe.wait_ge(w_lo, n + 1)
                for g in range(NB):
                    products(n, b, g)

            def tile_r(n, b):
                pe.wait_ge(w_lo, n + 1)
                for g in range(NB - 1):
                    products(n, b, g)
                for g in range(NB - 2):
                    turn_rows(n, b, g)
                products(n, b, NB - 1)
                for g in range(NB - 2, NB):
                    turn_rows(n, b, g)

            with pe.Fori(0, NTT // 2) as i:
                tile_t(2 * i, 0)
                tile_t(2 * i + 1, 1)
            with pe.Fori(0, NTR // 2) as i:
                tile_r(NTT + 2 * i, 0)
                tile_r(NTT + 2 * i + 1, 1)
            tile_t(NWT - 1, 0)


CH = 128
PJ = PAST // P


def gates(nc, d):
    with ExitStack() as ctx:
        sb, sem, psum = scope(nc, ctx)
        ident = sb("ident_g", [P, P])
        later = sb("later", [P, P])
        ones = sb("ones", [P, 1])
        unreset = sb("unreset", [P, NTOK])
        fl = sb("fl", [HEADS, NTOK])
        gg = sb("gg", [RANK, NTOK])
        wg2 = sb("wg2", [RANK, GKW])
        bf = sb("bf", [HEADS, 1])
        bg = sb("bg", [P, 2])
        pos = sb("pos", [P, 3, NTOK])
        neg = sb("neg", [P, 3, NTOK])
        run = sb("run", [P, 3, NTOK])
        fb = sb("fb", [HEADS, NTOK])
        frow = sb("frow", [TT, NT, HEADS])
        cl = sb("cl", [P, PJ, HEADS])
        incl = sb("incl", [P, HEADS, PJ])
        after = sb("after", [P, HEADS])
        suf = sb("suf", [P, PJ, HEADS])
        pb = sb("pb", [HEADS, PAST])
        ps = psum("ps_gates")
        filled, small_in, z_in, c_in = sem("filled_g"), sem("small_in"), sem("z_in"), sem("c_in")
        gate_done, soft, lows = sem("gate_done"), sem("soft"), sem("lows")
        logs, sums, biased = sem("logs"), sem("sums"), sem("biased")
        c_sum, c_after, c_suf = sem("c_sum"), sem("c_after"), sem("c_suf")
        s_later, s_turned, s_out, f_turned, f_out = sem("s_later"), sem("s_turned"), sem("s_out"), sem("f_turned"), sem("f_out")
        stored = sem("stored_g")
        block = ctx.enter_context(nc.Block())

        @block.sync
        def _(sp):
            sp.dma_start(gg[:], d["zT"][R_GG:R_GG + RANK, :]).then_inc(z_in, 16)
            sp.dma_start(fl[:], d["zT"][R_F:R_F + HEADS, :]).then_inc(z_in, 16)
            sp.dma_start(wg2[:], d["w_gate2"][0]).then_inc(small_in, 16)
            sp.dma_start(bg[:], d["b_gate2"][0].rearrange("(g p) -> p g", p=P), allow_slow_non_contiguous=True).then_inc(small_in, 16)
            sp.dma_start(bf[:], d["b_forget"][0].rearrange("(p a) -> p a", a=1), allow_slow_non_contiguous=True).then_inc(small_in, 16)
            sp.dma_start(cl[:], d["cache_fox_logf"][0, 0].rearrange("(p j) h -> p j h", j=PJ)).then_inc(c_in, 16)
            sp.wait_ge(s_out, 8)
            sp.dma_start(d["pbias"][:, :], pb[:]).then_inc(stored, 16)
            sp.wait_ge(f_out, 1)
            full = (NT - 1) * TT
            sp.dma_start(d["new_f_p"][0:full, :].rearrange("(t p) h -> p t h", p=TT), frow[:, 0:NT - 1, :]).then_inc(stored, 16)
            sp.dma_start(d["new_f_p"][full:SEQ, :], frow[0:LAST_PROMPT, NT - 1, :]).then_inc(stored, 16)
            sp.dma_start(d["new_f_s"][:, :], frow[LAST_PROMPT:TT, NT - 1, :]).then_inc(stored, 16)
            sp.wait_ge(biased, 1)
            sp.dma_start(d["kbias"][:, :], fb[:]).then_inc(stored, 16)
            sp.wait_ge(sums, 4)
            sp.dma_start(d["gsum"].rearrange("(g p) t -> p g t", p=P), run[:, 0:2, :]).then_inc(stored, 16)
            sp.wait_ge(stored, 16 * 6)

        @block.gpsimd
        def _(pool):
            fill_identity(pool, ident, filled)
            pool.memset(ones[:], 1.0).then_inc(filled, 1)
            pool.memset(later[:], 0.0).then_inc(filled, 1)
            pool.memset(unreset[:], 1.0).then_inc(filled, 1)
            pool.wait_ge(filled, 5)
            pool.affine_select(out=later[:], in_=later[:], compare_op=ALU.is_ge, fill=1.0, base=0,
                               pattern=[[1, P]], channel_multiplier=-1).then_inc(filled, 1)
            pool.memset(unreset[:, 0:NTOK:CH], 0.0).then_inc(filled, 1)

        @block.scalar
        def _(act):
            act.wait_ge(small_in, 48)
            act.wait_ge(z_in, 32)
            act.wait_ge(filled, 7)
            act.activation(pos[0:HEADS, 2], fl[:], ACT.Abs, bias=bf[:]).then_inc(soft, 1)
            for g in range(2):
                act.wait_ge(gate_done, NB * (g + 1))
                act.wait_ge(lows, NB * g + NB + 1)
                for b in range(NB):
                    act.activation(pos[:, g, b * BLK:(b + 1) * BLK], ps[:, b, 0:BLK], ACT.Abs, bias=bg[:, g:g + 1]).then_inc(soft, 1)
            act.wait_ge(soft, 2 * NB + 1)
            act.activation(pos[0:HEADS, 2], pos[0:HEADS, 2], ACT.Exp, scale=-1.0).then_inc(soft, 1)
            act.activation(pos[:, 0:2], pos[:, 0:2], ACT.Exp, scale=-1.0).then_inc(soft, 1)
            act.wait_ge(soft, 2 * NB + 3)
            act.activation(pos[0:HEADS, 2], pos[0:HEADS, 2], ACT.Ln, bias=ones[0:HEADS]).then_inc(logs, 1)
            act.activation(pos[:, 0:2], pos[:, 0:2], ACT.Ln, bias=ones[:]).then_inc(logs, 1)

        @block.tensor
        def _(pe):
            pe.wait_ge(small_in, 48)
            pe.wait_ge(z_in, 32)
            for g in range(2):
                for b in range(NB):
                    if g:
                        pe.wait_ge(soft, 1 + b + 1)
                    pe.matmul(ps[:, b, 0:BLK], wg2[:, g * P:(g + 1) * P], gg[:, b * BLK:(b + 1) * BLK],
                              start=True, stop=True).then_inc(gate_done, 1)
            pe.wait_ge(filled, 7)
            pe.wait_ge(c_sum, HEADS)
            pe.matmul(ps[:, 5, 0:HEADS], later[:], incl[:, :, PJ - 1], start=True, stop=True).then_inc(s_later, 1)
            pe.wait_ge(c_suf, 1)
            for r in range(8):
                if r >= 2:
                    pe.wait_ge(s_out, r - 1)
                for q in range(4):
                    j = 4 * r + q
                    last = pe.transpose(ps[0:HEADS, 6 + r % 2, q * P:(q + 1) * P], suf[:, j, :], ident[:])
                last.then_inc(s_turned, 1)
            pe.wait_ge(sums, 1)
            for t in range(NT):
                last = pe.transpose(ps[0:TT, 5, t * HEADS:(t + 1) * HEADS], neg[0:HEADS, 2, t * TT:(t + 1) * TT],
                                    ident[0:HEADS, 0:HEADS])
            last.then_inc(f_turned, 1)

        @block.vector
        def _(dve):
            dve.wait_ge(small_in, 48)
            dve.wait_ge(z_in, 32)
            dve.tensor_scalar(neg[0:HEADS, 2], fl[:], bf[:], 0.0, ALU.add, ALU.min).then_inc(lows, 1)
            for g in range(2):
                for b in range(NB):
                    dve.wait_ge(gate_done, NB * g + b + 1)
                    dve.tensor_scalar(neg[:, g, b * BLK:(b + 1) * BLK], ps[:, b, 0:BLK], bg[:, g:g + 1], 0.0,
                                      ALU.add, ALU.min).then_inc(lows, 1)
            dve.wait_ge(c_in, 16)
            dve.wait_ge(filled, 7)
            for h in range(HEADS):
                dve.tensor_tensor_scan(incl[:, h, :], ones[:].to_broadcast([P, PJ]), cl[:, :, h], 0.0,
                                       ALU.mult, ALU.add).then_inc(c_sum, 1)
            dve.wait_ge(s_later, 1)
            dve.wait_ge(c_sum, HEADS)
            dve.tensor_tensor(after[:], ps[:, 5, 0:HEADS], incl[:, :, PJ - 1], ALU.add).then_inc(c_after, 1)
            dve.wait_ge(c_after, 1)
            dve.tensor_tensor(suf[:].rearrange("p j h -> p h j"), after[:].unsqueeze(2).to_broadcast([P, HEADS, PJ]),
                              incl[:], ALU.subtract).then_inc(c_suf, 1)
            for r in range(8):
                dve.wait_ge(s_turned, r + 1)
                dve.tensor_scalar(pb[:, r * 512:(r + 1) * 512], ps[0:HEADS, 6 + r % 2, :], 1.0 / SCALE, None,
                                  ALU.mult).then_inc(s_out, 1)
            dve.wait_ge(logs, 1)
            dve.wait_ge(lows, 2 * NB + 1)
            dve.tensor_tensor(neg[0:HEADS, 2], neg[0:HEADS, 2], pos[0:HEADS, 2], ALU.subtract).then_inc(sums, 1)
            dve.wait_ge(sums, 1)
            dve.tensor_tensor_scan(run[0:HEADS, 2, 0:SEQ], ones[0:HEADS].to_broadcast([HEADS, SEQ]), neg[0:HEADS, 2, 0:SEQ],
                                   0.0, ALU.mult, ALU.add).then_inc(c_after, 1)
            dve.tensor_tensor_scan(run[0:HEADS, 2, SEQ:NTOK], ones[0:HEADS].to_broadcast([HEADS, NEW]), neg[0:HEADS, 2, SEQ:NTOK],
                                   0.0, ALU.mult, ALU.add).then_inc(c_after, 1)
            dve.wait_ge(c_after, 3)
            dve.tensor_scalar(fb[:], run[0:HEADS, 2], -1.0 / SCALE, None, ALU.mult).then_inc(biased, 1)
            dve.wait_ge(f_turned, 1)
            dve.tensor_copy(frow[:].rearrange("p t h -> p (t h)"), ps[0:TT, 5, 0:NT * HEADS]).then_inc(f_out, 1)
            dve.wait_ge(logs, 2)
            dve.tensor_tensor(neg[:, 0:2], neg[:, 0:2], pos[:, 0:2], ALU.subtract).then_inc(sums, 1)
            dve.wait_ge(sums, 2)
            for g in range(2):
                dve.tensor_tensor_scan(run[:, g], unreset[:], neg[:, g], 0.0, ALU.mult, ALU.add).then_inc(sums, 1)


QT = SEQ // P
NG = 4
GORDER = (3, 2, 1, 0)
UNITS = 2 * len(GORDER)
RING = 5
PT0, OB = 5, 7
BANKS_H = NG * sum(g + 1 for g in GORDER)
MASKED = -1.0e30


def chunk0(u, k):
    before = NG * sum(GORDER[v % 4] + 1 for v in range(u))
    return before + k * (GORDER[u % 4] + 1)


def parts(u, k):
    n = GORDER[u % 4] + 1
    return range(k * n, (k + 1) * n)


def group0(u):
    return NG * sum(GORDER[v % 4] + 1 for v in range(u))


def pair_rounds(e, both, score, part, final, split):
    def fused(it, u, it2, u2):
        for k in range(NG):
            both(it, u, it2, u2, k, (lambda: final(it2, u2 - 1)) if k == 0 and u2 else (lambda: None))

    def rest_of_pair(it, last):
        for u in range(1, UNITS):
            fused(it, u, it, u - 1)
            if u in (1, 2):
                split(2 * it + 1, 1, u - 1)
            if u in (5, 6) and not last:
                split(2 * it + 2, 0, u - 5)
    split(0, 0, 0)
    split(0, 0, 1)
    for k in range(NG):
        score(0, 0, k)
    with e.Fori(0, HEADS // 2 - 1) as it:
        rest_of_pair(it, False)
        fused(it + 1, 0, it, UNITS - 1)
        final(it, UNITS - 1)
    it = HEADS // 2 - 1
    rest_of_pair(it, True)
    final(it, UNITS - 2)
    for k in range(NG):
        part(it, UNITS - 1, k)
    final(it, UNITS - 1)


def fox_prompt(nc, d):
    with ExitStack() as ctx:
        sb, sem, psum = scope(nc, ctx)
        ident = sb("ident_f", [P, P])
        ident16 = sb("ident16", [P, P], BF16)
        mask16 = sb("mask16", [P, P], BF16)
        raw = sb("qk_raw", [HD + 1, 2, SEQ])
        qk = sb("qk_split", [HD + 1, 2, 2, 2, SEQ], F32R)
        va = sb("va", [P, 2, QT, HD + 1])
        pexp = sb("pexp", [P, 2, NG, SEQ])
        pt = sb("pt", [P, 2, 512])
        ot = sb("ot", [HD + 1, 512])
        tops = sb("tops", [P, 4])
        top = sb("top", [P, 1])
        ntop = sb("ntop", [P, 2, NG])
        rinv = sb("rinv", [P, NG])
        osb = sb("osb", [P, QT, 2 * HD])
        ps = psum("ps_fox")
        filled, ones_set = sem("filled_f"), sem("ones_set")
        raw_come, v_come = sem("raw_come"), [sem("v_come0"), sem("v_come1")]
        split_hi, split_lo = sem("split_hi"), sem("split_lo")
        scored, topped, joined, ntopped, expd = sem("scored"), sem("topped"), sem("joined"), sem("ntopped"), sem("expd")
        turned = sem("p_turned")
        pt_full = [sem("pt_full0"), sem("pt_full1")]
        summed, ot_full, o_turned = sem("o_summed"), sem("ot_full"), sem("o_turned")
        inverted, normed = sem("o_inverted"), sem("o_normed")
        stored, pairs = sem("stored_f"), sem("pairs")
        block = ctx.enter_context(nc.Block())
        EXP_CREDIT, PT_CREDIT, NORM_CREDIT, LO_CREDIT = RING, 1, 1, 1

        def nchunk(it, u, k):
            return 2 * BANKS_H * it + chunk0(u, k)

        def ntile(it, u, k):
            return NG * UNITS * it + NG * u + k

        def ngroup(it, u, j):
            return 2 * BANKS_H * it + group0(u) + j

        def half_group(it, u, j):
            return BANKS_H * it + (group0(u) + j) // 2 + 1

        def width(u, k, c):
            return 512 if c < GORDER[u % 4] else (k + 1) * P

        @block.sync
        def _(sp):
            def load_qk(h):
                sp.wait_ge(split_lo, 2 * h + LO_CREDIT)
                sp.dma_start(raw[0:HD, 0], d["zT"][bass.ds(h * HD + R_Q, HD), 0:SEQ]).then_inc(raw_come, 16)
                sp.dma_start(raw[0:HD, 1], d["zT"][bass.ds(h * HD + R_K, HD), 0:SEQ]).then_inc(raw_come, 16)
                sp.dma_start(raw[HD:HD + 1, 1], d["kbias"][bass.ds(h, 1), 0:SEQ]).then_inc(raw_come, 16)

            def load_v(col, b):
                sp.dma_start(va[:, b, :, 0:HD], d["new_v_p"].rearrange("(j p) c -> p j c", p=P)[:, :, bass.ds(col, HD)])\
                    .then_inc(v_come[b], 16)

            def store_pair(pair):
                sp.wait_ge(normed, UNITS * (pair + 1) + NORM_CREDIT)
                sp.sem_inc(pairs, 1)
                sp.dma_start(d["mixf"][0:SEQ, :].rearrange("(j p) c -> p j c", p=P)[:, :, bass.ds(pair * P, P)], osb[:])\
                    .then_inc(stored, 16)

            sp.sem_inc(stored, 16)
            sp.wait_ge(ones_set, 2)
            for h in range(2):
                load_qk(h)
                load_v(h * HD, h)
            with sp.Fori(0, HEADS // 2 - 1) as i:
                for b in range(2):
                    load_qk(2 * i + 2 + b)
                    sp.wait_ge(summed, 4 * (2 * i + b + 1))
                    load_v(i * (2 * HD) + (2 + b) * HD, b)
                store_pair(i)
            store_pair(HEADS // 2 - 1)
            sp.wait_ge(stored, 16 * (HEADS // 2 + 1))

        @block.gpsimd
        def _(pool):
            fill_identity(pool, ident, filled)
            pool.memset(ident16[:], 0.0).then_inc(filled, 1)
            pool.memset(mask16[:], 0.0).then_inc(filled, 1)
            pool.wait_ge(filled, 4)
            pool.affine_select(out=ident16[:], in_=ident16[:], compare_op=ALU.not_equal, fill=1.0, base=0,
                               pattern=[[-1, P]], channel_multiplier=1).then_inc(filled, 1)
            pool.affine_select(out=mask16[:], in_=mask16[:], compare_op=ALU.is_ge, fill=MASKED, base=0,
                               pattern=[[-1, P]], channel_multiplier=1).then_inc(filled, 1)

        @block.tensor
        def _(pe):
            pe.wait_ge(filled, 6)

            def score(it, u, k):
                b, G = u // 4, GORDER[u % 4]
                if u % 4 == 0 and k == 0:
                    pe.wait_ge(split_lo, 4 * it + 2 * b + 2 + LO_CREDIT)
                i = NG * G + k
                for c in range(G + 1):
                    n = nchunk(it, u, k) + c
                    bank = (chunk0(u, k) + c) % RING
                    w = width(u, k, c)
                    pe.wait_ge(expd, n - RING + 1 + EXP_CREDIT)
                    for m, (s, v) in enumerate(PASSES):
                        last = pe.matmul(ps[:, bank, 0:w], qk[:, b, s, 0, i * P:(i + 1) * P],
                                         qk[:, b, v, 1, 512 * c:512 * c + w], start=m == 0, stop=m == 2 and c < G)
                    if c == G:
                        last = pe.matmul(ps[:, bank, w - P:w], ident16[:], mask16[:], start=False, stop=True)
                    last.then_inc(scored, 1)

            def times_v(it, u, j):
                b, G = u // 4, GORDER[u % 4]
                q0 = max(0, j - NG * G) * P
                par = (group0(u) + j) % 2
                pe.wait_ge(pt_full[par], half_group(it, u, j) + PT_CREDIT)
                if j == 0:
                    pe.wait_ge(normed, UNITS * it + u + NORM_CREDIT)
                    if u % 4 == 0:
                        pe.wait_ge(v_come[b], 16 * it + 16)
                return pe.matmul(ps[0:HD + 1, OB, q0:512], va[:, b, j, :], pt[:, par, q0:512],
                                 start=j == 0, stop=j == NG * G + 3)

            def part(it, u, k):
                G = GORDER[u % 4]
                for j in parts(u, k):
                    par = (group0(u) + j) % 2
                    pe.wait_ge(pt_full[par], half_group(it, u, j) - 1 + PT_CREDIT)
                    if j == 0:
                        pe.wait_ge(expd, nchunk(it, u, NG) + EXP_CREDIT)
                    for q in range(max(0, j - NG * G), NG):
                        last = pe.transpose(ps[:, PT0 + par, q * P:(q + 1) * P], pexp[:, u % 2, q, j * P:(j + 1) * P], ident[:])
                    last.then_inc(turned, 1)
                    if j:
                        times_v(it, u, j - 1)
                if k == 3:
                    times_v(it, u, NG * G + 3).then_inc(summed, 1)

            def final(it, u):
                pe.wait_ge(ot_full, UNITS * it + u + 1)
                for q in range(NG):
                    last = pe.transpose(ps[:, OB, q * (HD + 1):(q + 1) * (HD + 1)], ot[:, q * P:(q + 1) * P],
                                        ident[0:HD + 1, 0:HD + 1])
                last.then_inc(o_turned, 1)

            def both(it, u, it2, u2, k, outputs):
                score(it, u, k)
                outputs()
                part(it2, u2, k)

            pair_rounds(pe, both, score, part, final, lambda h, b, p: None)

        @block.scalar
        def _(act):
            act.sem_inc(expd, EXP_CREDIT)
            act.sem_inc(pt_full[0], PT_CREDIT)

            def exp(it, u, k, c):
                w = width(u, k, c)
                act.activation(pexp[:, u % 2, k, 512 * c:512 * c + w], ps[:, (chunk0(u, k) + c) % RING, 0:w], ACT.Exp,
                               bias=ntop[:, u % 2, k:k + 1], scale=SCALE).then_inc(expd, 1)

            def copy(it, u, j):
                q0 = max(0, j - NG * GORDER[u % 4]) * P
                act.wait_ge(turned, ngroup(it, u, j) + 1)
                act.activation(pt[:, 0, q0:512], ps[:, PT0, q0:512], ACT.Copy).then_inc(pt_full[0], 1)

            def even(u, k):
                return [j for j in parts(u, k) if (group0(u) + j) % 2 == 0]

            def both(it, u, it2, u2, k, outputs):
                js, cs = even(u2, k), range(GORDER[u % 4] + 1)
                for n in range(max(len(js), len(cs))):
                    if n < len(js):
                        copy(it2, u2, js[n])
                    if n == 0:
                        act.wait_ge(ntopped, ntile(it, u, k) + 1)
                    if n < len(cs):
                        exp(it, u, k, n)

            def score(it, u, k):
                act.wait_ge(ntopped, ntile(it, u, k) + 1)
                for c in range(GORDER[u % 4] + 1):
                    exp(it, u, k, c)

            def part(it, u, k):
                for j in even(u, k):
                    copy(it, u, j)

            def split(h, b, p):
                act.wait_ge(raw_come, 48 * h + 48)
                act.activation(qk[:, b, HI, p], raw[:, p], ACT.Copy).then_inc(split_hi, 1)

            pair_rounds(act, both, score, part, lambda it, u: None, split)

        @block.vector
        def _(dve):
            dve.sem_inc(pt_full[1], PT_CREDIT)
            dve.sem_inc(normed, NORM_CREDIT)
            dve.sem_inc(split_lo, LO_CREDIT)
            dve.memset(raw[HD:HD + 1, 0], 1.0).then_inc(ones_set, 1)
            dve.memset(va[:, :, :, HD:HD + 1], 1.0).then_inc(ones_set, 1)

            def score(it, u, k):
                G = GORDER[u % 4]
                for c in range(G + 1):
                    n = nchunk(it, u, k) + c
                    dve.wait_ge(scored, n + 1)
                    dve.reduce_max(tops[:, c:c + 1], ps[:, (chunk0(u, k) + c) % RING, 0:width(u, k, c)], AX.X).then_inc(topped, 1)
                dve.wait_ge(topped, nchunk(it, u, k) + G + 1)
                dve.reduce_max(top[:], tops[:, 0:G + 1], AX.X).then_inc(joined, 1)
                dve.wait_ge(joined, ntile(it, u, k) + 1)
                dve.tensor_scalar(ntop[:, u % 2, k:k + 1], top[:], -SCALE, None, ALU.mult).then_inc(ntopped, 1)

            def part(it, u, k):
                G = GORDER[u % 4]
                for j in parts(u, k):
                    if (group0(u) + j) % 2:
                        q0 = max(0, j - NG * G) * P
                        dve.wait_ge(turned, ngroup(it, u, j) + 1)
                        dve.tensor_copy(pt[:, 1, q0:512], ps[:, PT0 + 1, q0:512]).then_inc(pt_full[1], 1)
                if k == 3:
                    dve.wait_ge(summed, UNITS * it + u + 1)
                    dve.tensor_copy(ot[:], ps[0:HD + 1, OB, :]).then_inc(ot_full, 1)

            def final(it, u):
                b, G = u // 4, GORDER[u % 4]
                n = UNITS * it + u
                dve.wait_ge(o_turned, n + 1)
                rows = ps[:, OB, 0:NG * (HD + 1)].rearrange("p (q c) -> p q c", q=NG)
                dve.reciprocal(rinv[:], rows[:, :, HD]).then_inc(inverted, 1)
                dve.wait_ge(inverted, n + 1)
                if u == 0:
                    dve.wait_ge(stored, 16 * it + 16)
                dve.tensor_tensor(osb[:, NG * G:NG * (G + 1), b * HD:(b + 1) * HD], rows[:, :, 0:HD],
                                  rinv[:].unsqueeze(2).to_broadcast([P, NG, HD]), ALU.mult).then_inc(normed, 1)

            def split(h, b, p):
                dve.wait_ge(split_hi, 2 * h + p + 1)
                dve.tensor_tensor(qk[:, b, LO, p], raw[:, p], qk[:, b, HI, p].bitcast(F32), ALU.subtract).then_inc(split_lo, 1)

            def both(it, u, it2, u2, k, outputs):
                score(it, u, k)
                outputs()
                part(it2, u2, k)

            pair_rounds(dve, both, score, part, final, split)

NGR = 2
HG = HEADS // NGR
NCK = PAST // 512
KEYS = PAST + NEW


def fox_sample(nc, d):
    with ExitStack() as ctx:
        sb, sem, psum = scope(nc, ctx)
        ident = sb("ident_s", [P, P])
        spread = sb("spread", [NEW, P], BF16)
        mask16 = sb("mask_s", [NEW, NEW], BF16)
        kc = sb("kc", [P, PJ, FOX])
        vc = sb("vc", [P, PJ, FOX])
        kn = sb("kn", [P, HEADS // 2, NEW])
        vn = sb("vn", [NEW, FOX])
        qb = sb("qb", [P, HEADS // 2, P])
        kt = sb("kt", [P, 2, 2, 512])
        s = sb("s", [P, NGR, KEYS])
        pt = sb("pt_s", [P, 2, 512])
        tops = sb("tops_s", [P, NGR, NCK + 1])
        top = sb("top_s", [P, NGR])
        ntop = sb("ntop_s", [P, NGR])
        sums = sb("sums_s", [P, NGR])
        rinv = sb("rinv_s", [P, NGR])
        osb = sb("osb_s", [P, NGR, HD])
        ps = psum("ps_fs")
        filled, zeroed, q_in, n_in, bias_in = (
            sem("filled_s"), sem("zeroed_s"), sem("q_in"), sem("n_in"), [sem(f"bias_in{g}") for g in range(NGR)])
        k_in = [sem(f"k_in{c}") for c in range(NCK)]
        v_in = [sem(f"v_in{c}") for c in range(NCK)]
        k_turned, kt_even, kt_odd, scored, summed = sem("k_turned"), sem("kt_even"), sem("kt_odd"), sem("scored_s"), sem("summed_s")
        topped, joined, ntopped, expd = sem("topped_s"), sem("joined_s"), sem("ntopped_s"), sem("expd_s")
        p_turned, pt_full, o_done, inverted, o_out, stored = (
            sem("p_turned_s"), [sem("pt_full_s0"), sem("pt_full_s1")], sem("o_done_s"), sem("inverted_s"), sem("o_out_s"), sem("stored_s"))
        block = ctx.enter_context(nc.Block())
        TK, SC, TP, OB_S = 0, 2, 4, 6
        NPT = NCK + 1

        @block.sync
        def _(sp):
            ck = d["cache_fox_k"][0, 0].rearrange("(p j) h c -> p j (h c)", j=PJ)
            cv = d["cache_fox_v"][0, 0].rearrange("(p j) h c -> p j (h c)", j=PJ)
            for c in range(2):
                sp.dma_start(kc[:, 4 * c:4 * c + 4], ck[:, 4 * c:4 * c + 4]).then_inc(k_in[c], 16)
            sp.wait_ge(zeroed, 1)
            for h in range(HEADS):
                g, e = h // 2, h % 2
                col = (h % HG) * NEW
                sp.dma_start(qb[e * HD:(e + 1) * HD, g, col:col + NEW], d["zT"][R_Q + h * HD:R_Q + (h + 1) * HD, SEQ:NTOK]).then_inc(q_in, 16)
            for c in range(2, NCK):
                sp.dma_start(kc[:, 4 * c:4 * c + 4], ck[:, 4 * c:4 * c + 4]).then_inc(k_in[c], 16)
            for c in range(NCK):
                sp.dma_start(vc[:, 4 * c:4 * c + 4], cv[:, 4 * c:4 * c + 4]).then_inc(v_in[c], 16)
            for h in range(HEADS):
                g, hh = divmod(h, HG)
                if hh == 0:
                    sp.wait_ge(o_out, HG * (g + 1))
                sp.dma_start(d["mixf"][SEQ:NTOK, h * HD:(h + 1) * HD], osb[hh * NEW:(hh + 1) * NEW, g, :]).then_inc(stored, 16)
            sp.wait_ge(stored, 16 * HEADS)

        @block.gpsimd
        def _(pool):
            fill_identity(pool, ident, filled)
            pool.memset(spread[:], 0.0).then_inc(filled, 1)
            pool.memset(mask16[:], 0.0).then_inc(filled, 1)
            pool.wait_ge(filled, 4)
            pool.affine_select(out=spread[:].rearrange("p (h q) -> p h q", q=NEW), in_=spread[:].rearrange("p (h q) -> p h q", q=NEW),
                               compare_op=ALU.not_equal, fill=1.0, base=0, pattern=[[0, HG], [-1, NEW]], channel_multiplier=1).then_inc(filled, 1)
            pool.affine_select(out=mask16[:], in_=mask16[:], compare_op=ALU.is_ge, fill=MASKED, base=0,
                               pattern=[[-1, NEW]], channel_multiplier=1).then_inc(filled, 1)

        @block.tensor
        def _(pe):
            pe.wait_ge(filled, 6)

            def turn_keys(g, c):
                n = NCK * g + c
                if g == 0:
                    pe.wait_ge(k_in[c], 16)
                for pr in range(2):
                    if n:
                        pe.wait_ge(kt_odd if pr else kt_even, n)
                    for q in range(4):
                        last = pe.transpose(ps[:, TK + pr, q * P:(q + 1) * P], kc[:, 4 * c + q, (2 * g + pr) * P:(2 * g + pr + 1) * P], ident[:])
                    last.then_inc(k_turned, 1)

            def score(g, c):
                n = NPT * g + c
                if n >= 2:
                    pe.wait_ge(summed, n - 1)
                bank = SC + n % 2
                if c < NCK:
                    pe.wait_ge(kt_even, NCK * g + c + 1)
                    pe.wait_ge(kt_odd, NCK * g + c + 1)
                    for pr in range(2):
                        last = pe.matmul(ps[:, bank, :], qb[:, 2 * g + pr, :], kt[:, c % 2, pr, :], start=pr == 0, stop=pr == 1)
                else:
                    pe.wait_ge(n_in, 32)
                    for pr in range(2):
                        pe.matmul(ps[:, bank, 0:NEW], qb[:, 2 * g + pr, :], kn[:, 2 * g + pr, :], start=pr == 0, stop=False)
                    last = pe.matmul(ps[:, bank, 0:NEW], spread[:], mask16[:], start=False, stop=True)
                last.then_inc(scored, 1)

            def turn_exps(g, c):
                n = NPT * g + c
                if n >= 2:
                    pe.wait_ge(pt_full[n % 2], n // 2)
                w = 4 if c < NCK else 1
                for q in range(w):
                    keys = P if c < NCK else NEW
                    col = 512 * c + q * P
                    last = pe.transpose(ps[0:keys, TP + n % 2, q * P:(q + 1) * P], s[:, g, col:col + keys], ident[:])
                last.then_inc(p_turned, 1)

            def times_v(g, c):
                n = NPT * g + c
                pe.wait_ge(pt_full[n % 2], n // 2 + 1)
                out, vcols = ps[:, OB_S + g, 0:HG * HD], slice(g * HG * HD, (g + 1) * HG * HD)
                if c < NCK:
                    if g == 0:
                        pe.wait_ge(v_in[c], 16)
                    for q in range(4):
                        pe.matmul(out, pt[:, n % 2, q * P:(q + 1) * P], vc[:, 4 * c + q, vcols], start=c == 0 and q == 0, stop=False)
                else:
                    pe.matmul(out, pt[0:NEW, n % 2, 0:P], vn[:, vcols], start=False, stop=True).then_inc(o_done, 1)

            for g in range(NGR):
                turn_keys(g, 0)
                if g == 0:
                    pe.wait_ge(q_in, 16 * HEADS)
                for c in range(NPT):
                    if c + 1 < NCK:
                        turn_keys(g, c + 1)
                    score(g, c)
            for g in range(NGR):
                pe.wait_ge(expd, g + 1)
                turn_exps(g, 0)
                for c in range(NPT):
                    if c + 1 < NPT:
                        turn_exps(g, c + 1)
                    times_v(g, c)

        def copy_exps(e, copy, g, c):
            n = NPT * g + c
            e.wait_ge(p_turned, n + 1)
            w, keys = (512, P) if c < NCK else (P, NEW)
            copy(pt[0:keys, n % 2, 0:w], ps[0:keys, TP + n % 2, 0:w]).then_inc(pt_full[n % 2], 1)

        @block.scalar
        def _(act):
            for h in range(HEADS):
                g, hh = divmod(h, HG)
                rows = slice(hh * NEW, (hh + 1) * NEW)
                act.dma_start(s[rows, g, 0:PAST], d["pbias"][h, :].partition_broadcast(NEW)).then_inc(bias_in[g], 16)
                act.dma_start(s[rows, g, PAST:KEYS], d["kbias"][h, SEQ:NTOK].partition_broadcast(NEW)).then_inc(bias_in[g], 16)
            act.dma_start(kn[:], d["zT"][R_K:R_K + FOX, SEQ:NTOK].rearrange("(g p) t -> p g t", p=P)).then_inc(n_in, 16)
            act.dma_start(vn[:], d["new_v_s"]).then_inc(n_in, 16)

            def exp(g):
                act.wait_ge(ntopped, g + 1)
                act.wait_ge(summed, NPT * (g + 1))
                act.activation(s[:, g], s[:, g], ACT.Exp, bias=ntop[:, g:g + 1], scale=SCALE, accum_out=sums[:, g:g + 1]).then_inc(expd, 1)

            for g in range(NGR):
                for c in range(NCK):
                    n = NCK * g + c
                    if g == 1 and c == 2:
                        exp(0)
                    act.wait_ge(k_turned, 2 * n + 1)
                    if n >= 2:
                        act.wait_ge(scored, NPT * ((n - 2) // NCK) + (n - 2) % NCK + 1)
                    act.activation(kt[:, c % 2, 0], ps[:, TK, :], ACT.Copy).then_inc(kt_even, 1)
            exp(1)
            for n in range(0, NPT * NGR, 2):
                copy_exps(act, lambda o, i: act.activation(o, i, ACT.Copy), *divmod(n, NPT))

        @block.vector
        def _(dve):
            dve.memset(qb[:], 0.0).then_inc(zeroed, 1)

            def copy_keys(n):
                dve.wait_ge(k_turned, 2 * n + 2)
                if n >= 2:
                    dve.wait_ge(scored, NPT * ((n - 2) // NCK) + (n - 2) % NCK + 1)
                dve.tensor_copy(kt[:, n % 2, 1], ps[:, TK + 1, :]).then_inc(kt_odd, 1)

            for g in range(NGR):
                copy_keys(NCK * g)
                for c in range(NPT):
                    n = NPT * g + c
                    if c + 1 < NCK:
                        copy_keys(NCK * g + c + 1)
                    if c == 0:
                        dve.wait_ge(bias_in[g], 32 * HG)
                    dve.wait_ge(scored, n + 1)
                    cols = slice(512 * c, 512 * (c + 1) if c < NCK else KEYS)
                    w = 512 if c < NCK else NEW
                    dve.tensor_tensor(s[:, g, cols], ps[:, SC + n % 2, 0:w], s[:, g, cols], ALU.add).then_inc(summed, 1)
                    dve.wait_ge(summed, n + 1)
                    dve.reduce_max(tops[:, g, c:c + 1], s[:, g, cols], AX.X).then_inc(topped, 1)
                dve.wait_ge(topped, NPT * (g + 1))
                dve.reduce_max(top[:, g:g + 1], tops[:, g], AX.X).then_inc(joined, 1)
                dve.wait_ge(joined, g + 1)
                dve.tensor_scalar(ntop[:, g:g + 1], top[:, g:g + 1], -SCALE, None, ALU.mult).then_inc(ntopped, 1)
            def norm(g):
                dve.wait_ge(expd, g + 1)
                dve.reciprocal(rinv[:, g:g + 1], sums[:, g:g + 1]).then_inc(inverted, 1)
                dve.wait_ge(inverted, g + 1)
                dve.wait_ge(o_done, g + 1)
                for hh in range(HG):
                    rows = slice(hh * NEW, (hh + 1) * NEW)
                    dve.tensor_scalar(osb[rows, g, :], ps[rows, OB_S + g, hh * HD:(hh + 1) * HD], rinv[rows, g:g + 1], None, ALU.mult).then_inc(o_out, 1)

            for n in range(1, NPT * NGR, 2):
                copy_exps(dve, dve.tensor_copy, *divmod(n, NPT))
                if n == NPT + 4:
                    norm(0)
            norm(1)


HALVES = (64, 32, 16, 8, 4, 2, 1)
NL = len(HALVES)
E_B, E_K = NL, NL + 1
Q_RAW = NL + 1
NCH = SEQ // CH


def gla(nc, d):
    with ExitStack() as ctx:
        sb, sem, psum = scope(nc, ctx)
        ident = sb("ident_l", [P, P])
        masks = sb("masks", [P, NL, CH // 2])
        qe = sb("qe", [P, 2, NL + 2, 2, 2, CH])
        kr = sb("kr", [P, 2, 2, CH])
        bs = sb("bs", [P, 2, 2, CH])
        vs = sb("vs", [P, 2, GVW])
        gr = sb("gr", [P, 2, GVW])
        gn = sb("gn", [P, GVW])
        ex = sb("ex", [P, 2, NL + 2, 2, CH])
        ke = sb("ke", [P, 2, NL, 2, CH])
        kd = sb("kd", [P, 2, 2, CH])
        kdt = sb("kdt", [P, 2 * P])
        att = sb("att", [P, GH, CH])
        eg = sb("eg", [P, 2, GVW])
        sg = sb("sg", [P, 2, GVW])
        ov = sb("ov", [P, 2, GVW])
        sq = sb("sq", [P, GH, GV])
        og = sb("og", [P, 2, GVW])
        osq = sb("osq", [P, 2, GH])
        st = sb("st", [P, 2, GV])
        tick = sb("tick", [P, 1])
        ones = sb("ones_l", [P, 1])
        ps = psum("ps_gla")
        filled, g_in, zeroed = sem("filled_l"), sem("gn_in"), sem("zeroed")
        g_come = [sem("g_come0"), sem("g_come1")]
        k_come = [sem("k_come0"), sem("k_come1")]
        vl_come = [sem("vl_come0"), sem("vl_come1")]
        turns = sem("turns")
        st_in, st_set, st_stored = sem("st_in"), sem("st_set"), sem("st_stored")
        uppers, lowers, decays = sem("uppers"), sem("lowers"), sem("decays")
        k_ready, q_ready0, q_ready1 = sem("k_ready"), sem("q_ready0"), sem("q_ready1")
        g_exp, g_log, g_inv, g_mul, g_ready = sem("g_exp"), sem("g_log"), sem("g_inv"), sem("g_mul"), sem("g_ready")
        p_done, kd_out, level_picked, picked = sem("p_done"), sem("kd_out"), sem("level_picked"), sem("picked")
        o_done, kv_done, o_out, o_sq, st_new = sem("o_done"), sem("kv_done"), sem("o_out"), sem("o_sq"), sem("st_new")
        gated, stored = sem("gated"), [sem("stored_l0"), sem("stored_l1")]
        block = ctx.enter_context(nc.Block())
        CREDIT = 2

        def levels(L):
            return [(l, h) for l, h in enumerate(HALVES) if 2 * h <= L]

        def halved(ap, half):
            names = {3: "p g (n a h) -> p g n a h"}
            return ap.rearrange(names[len(ap.shape)], a=2, h=half)

        @block.sync
        def _(sp):
            for b in range(2):
                sp.sem_inc(stored[b], 32)
            sp.dma_start(gn[:], d["gla_norm_g"].partition_broadcast(P)).then_inc(g_in, 16)
            sp.dma_start(st[:], d["state_gla"][0, 0].rearrange("(g e) k v -> (e k) g v", e=2)).then_inc(st_in, 16)

            def load_g(b, L, tok):
                sp.dma_start(bs[:, b, :, 0:L], d["gsum"][:, bass.ds(tok, L)].rearrange("(g p) t -> p g t", p=P)).then_inc(g_come[b], 16)
                sp.dma_start(gr[0:L, b], d["zrow"][bass.ds(tok, L), GVW:2 * GVW]).then_inc(g_come[b], 16)

            def load_k(b, L, tok):
                for e in range(2):
                    sp.dma_start(qe[e * GK:(e + 1) * GK, b, Q_RAW, :, e, 0:L],
                                 d["zT"][R_GQ:R_GQ + GKW, bass.ds(tok, L)].rearrange("(g e k) t -> e k g t", e=2, k=GK)[e])\
                        .then_inc(k_come[b], 16)
                sp.dma_start(kr[:, b, :, 0:L], d["zT"][R_GK:R_GK + GKW, bass.ds(tok, L)].rearrange("(g p) t -> p g t", p=P)).then_inc(k_come[b], 16)

            def load_v(b, L, tok):
                sp.dma_start(vs[0:L, b], d["zrow"][bass.ds(tok, L), 0:GVW]).then_inc(vl_come[b], 16)

            def store(t, b, L, tok):
                sp.wait_ge(gated, t + 2 + CREDIT)
                sp.dma_start(d["mixg"][bass.ds(tok, L), :], og[0:L, b]).then_inc(stored[b], 16)
                sp.dma_start(d["gsq"][bass.ds(tok, L), :], osq[0:L, b]).then_inc(stored[b], 16)

            def turn(t, b, before=None):
                tok = (t + 2) * CH
                sp.wait_ge(g_mul, t + 2)
                load_g(b, CH, tok)
                sp.wait_ge(p_done, t + 2)
                load_k(b, CH, tok)
                if before:
                    store(t - 1, 1 - b, *before)
                sp.wait_ge(kv_done, t + 2)
                sp.sem_inc(turns, 1)
                load_v(b, CH, tok)

            for b, L, tok in ((1, NEW, SEQ), (0, CH, 0)):
                load_g(b, L, tok)
                if b:
                    sp.wait_ge(zeroed, 4)
                load_k(b, L, tok)
                load_v(b, L, tok)
            turn(-1, 1)
            sp.wait_ge(st_new, 4)
            sp.dma_start(d["st_s"].rearrange("(g p) v -> p g v", p=P), st[:]).then_inc(st_stored, 16)
            turn(0, 0, (NEW, SEQ))
            with sp.Fori(0, (NCH - 4) // 2) as i:
                turn(2 * i + 1, 1, (CH, 2 * i * CH))
                turn(2 * i + 2, 0, (CH, (2 * i + 1) * CH))
            turn(NCH - 3, 1, (CH, (NCH - 4) * CH))
            for t in range(NCH - 3, NCH):
                store(t, t % 2, CH, t * CH)
            sp.wait_ge(st_new, 4 * (NCH + 1))
            sp.dma_start(d["st_p"].rearrange("(g p) v -> p g v", p=P), st[:]).then_inc(st_stored, 16)
            for b in range(2):
                sp.wait_ge(stored[b], 32 * (NCH // 2 + 1 + b))
            sp.wait_ge(st_stored, 32)

        def run(e, front, back, between):
            front(-1, 1, NEW)
            back(-1, 1, NEW)
            between()
            skewed(e, NCH, lambda t, b: front(t, b, CH), lambda t, b: back(t, b, CH))

        def stored_before(t, b):
            return 16 * (t - b) + 32 + 32 * b

        def came(t, b, loads):
            return 8 * loads * (t - b) + 16 * loads * (1 + b)

        @block.gpsimd
        def _(pool):
            fill_identity(pool, ident, filled)
            pool.memset(masks[:], 1.0).then_inc(filled, 1)
            pool.wait_ge(filled, 3)
            n = 3
            for l, half in enumerate(HALVES):
                m = masks[:, l, :].rearrange("p (n h) -> p n h", h=half)
                nb = CH // (2 * half)
                pool.affine_select(out=m, in_=m, compare_op=ALU.is_ge, fill=0.0, base=0,
                                   pattern=[[-2 * half, nb], [0, half]], channel_multiplier=1).then_inc(filled, 1)
                n += 1
                pool.wait_ge(filled, n)
                pool.affine_select(out=m, in_=m, compare_op=ALU.is_ge, fill=0.0, base=half - 1,
                                   pattern=[[2 * half, nb], [0, half]], channel_multiplier=-1).then_inc(filled, 1)
                n += 1
                pool.wait_ge(filled, n)
            pool.wait_ge(g_in, 16)
            pool.wait_ge(zeroed, 5)

            def front(t, b, L):
                pool.wait_ge(g_come[b], came(t, b, 2))
                if not isinstance(t, int) or t >= 0:
                    pool.wait_ge(g_ready, t + 1)
                for l, half in levels(L):
                    bh = halved(bs[:, b, :, 0:L], half)
                    xh = halved(ex[:, b, l, :, 0:L], half)
                    last = pool.tensor_tensor(xh[:, :, :, 0, :], bh[:, :, :, 0, half - 1:half].to_broadcast([P, 2, L // (2 * half), half]),
                                              bh[:, :, :, 0, :], ALU.subtract)
                last.then_inc(lowers, 1)
                pool.wait_ge(decays, 2 * (t + 2))
                pool.wait_ge(k_come[b], came(t, b, 3))
                if not isinstance(t, int) or t >= 1:
                    pool.wait_ge(kv_done, t)
                l0 = levels(L)[0][0]
                n = NL + 1 - l0
                pool.tensor_tensor(qe[GK:P, b, l0:NL + 1, :, 1, 0:L],
                                   qe[GK:P, b, Q_RAW:Q_RAW + 1, :, 1, 0:L].to_broadcast([GK, n, 2, L]),
                                   ex[GK:P, b, l0:NL + 1, :, 0:L], ALU.mult).then_inc(q_ready1, 1)
                pool.wait_ge(q_ready1, t + 2)
                pool.wait_ge(g_inv, t + 2)
                pool.wait_ge(gated, t + CREDIT)
                pool.tensor_tensor(sg[0:L, b], gr[0:L, b], eg[0:L, b], ALU.mult).then_inc(g_mul, 1)
                pool.wait_ge(g_mul, t + 2)
                pool.tensor_tensor(sg[0:L, b], sg[0:L, b], gn[0:L], ALU.mult).then_inc(g_ready, 1)

            run(pool, front, lambda t, b, L: None, lambda: None)

        @block.scalar
        def _(act):
            act.wait_ge(zeroed, 5)
            def front(t, b, L):
                l0 = levels(L)[0][0]
                act.wait_ge(g_come[b], came(t, b, 2))
                if not isinstance(t, int) or t >= 1:
                    act.wait_ge(st_new, 4 * t)
                    act.wait_ge(g_ready, t)
                act.activation(ex[:, b, E_B, :, 0:L], bs[:, b, :, 0:L], ACT.Exp, scale=1.0 / TEMP).then_inc(decays, 1)
                act.activation(eg[0:L, b], gr[0:L, b], ACT.Exp, scale=-1.0).then_inc(g_exp, 1)
                act.wait_ge(g_exp, t + 2)
                act.activation(eg[0:L, b], eg[0:L, b], ACT.Ln, bias=ones[0:L]).then_inc(g_log, 1)
                act.wait_ge(g_log, t + 2)
                act.activation(eg[0:L, b], eg[0:L, b], ACT.Exp, scale=-1.0).then_inc(g_inv, 1)
                act.wait_ge(uppers, t + 2)
                act.wait_ge(lowers, t + 2)
                act.activation(ex[:, b, l0:NL, :, 0:L], ex[:, b, l0:NL, :, 0:L], ACT.Exp, scale=1.0 / TEMP)
                act.activation(ex[:, b, E_K, :, 0:L], ex[:, b, E_K, :, 0:L], ACT.Exp, scale=1.0 / TEMP).then_inc(decays, 1)

            def back(t, b, L):
                act.wait_ge(p_done, t + 2)
                act.activation(kdt[0:L], ps[0:L, 6, 0:2 * P], ACT.Copy).then_inc(kd_out, 1)
                act.wait_ge(o_done, t + 2)
                act.activation(ov[0:L, b], ps[0:L, 5, :], ACT.Copy, scale=GK ** -0.5).then_inc(o_out, 1)
                act.wait_ge(o_out, t + 2)
                act.wait_ge(stored[b], stored_before(t, b))
                if not isinstance(t, int) or t >= 0:
                    act.wait_ge(o_sq, GH * (t + 1))
                for h in range(GH):
                    act.activation(sq[0:L, h], ov[0:L, b, h * GV:(h + 1) * GV], ACT.Square, accum_out=osq[0:L, b, h:h + 1]).then_inc(o_sq, 1)

            run(act, front, back, lambda: None)

        @block.tensor
        def _(pe):
            pe.wait_ge(filled, 3 + 2 * NL)
            pe.wait_ge(zeroed, 4)

            def back(t, b, L):
                pe.wait_ge(k_ready, 2 * (t + 2))
                pe.wait_ge(q_ready0, t + 2)
                pe.wait_ge(q_ready1, t + 2)
                if not isinstance(t, int) or t >= 0:
                    pe.wait_ge(picked, (t + 1))
                    pe.wait_ge(kd_out, t + 1)
                for l, half in levels(L):
                    for g in range(2):
                        c = (l % 2) * 256 + g * 128
                        pe.matmul(ps[0:L, l // 2, c:c + 128].rearrange("p (e t) -> p e t", e=2)[:, :, 0:L // 2],
                                  ke[:, b, l, g, 0:L],
                                  halved(qe[:, b, l, g, :, 0:L], half)[:, :, :, 1, :], start=True, stop=True)
                for g in range(2):
                    pe.matmul(ps[0:L, 4, g * 256:(g + 1) * 256].rearrange("p (e t) -> p e t", e=2)[:, :, 0:L],
                              kr[:, b, g, 0:L], qe[:, b, Q_RAW, g, :, 0:L], start=True, stop=True)
                for g in range(2):
                    last = pe.transpose(ps[0:L, 6, g * P:(g + 1) * P], kd[:, b, g, 0:L], ident[:])
                last.then_inc(p_done, 1)
                pe.wait_ge(picked, t + 2)
                pe.wait_ge(vl_come[b], came(t, b, 1))
                if isinstance(t, int) and t <= 0:
                    pe.wait_ge(st_set, t + 2)
                if not isinstance(t, int) or t > 0:
                    pe.wait_ge(st_new, 4 * (t + 1))
                if not isinstance(t, int) or t >= 0:
                    pe.wait_ge(o_out, t + 1)
                for h in range(GH):
                    g, e = divmod(h, 2)
                    o = ps[0:L, 5, h * GV:(h + 1) * GV]
                    pe.matmul(o, att[0:L, h, 0:L], vs[0:L, b, h * GV:(h + 1) * GV], start=True, stop=False)
                    last = pe.matmul(o, qe[:, b, E_B, g, e, 0:L], st[:, g, :], start=False, stop=True)
                last.then_inc(o_done, 1)
                pe.wait_ge(kd_out, t + 2)
                for g in range(2):
                    last = pe.matmul(ps[:, 7, g * 256:(g + 1) * 256], kdt[0:L, g * P:(g + 1) * P],
                                     vs[0:L, b, g * 256:(g + 1) * 256], start=True, stop=True)
                last.then_inc(kv_done, 1)

            run(pe, lambda t, b, L: None, back, lambda: None)

        @block.vector
        def _(dve):
            dve.sem_inc(gated, CREDIT)
            for b in range(2):
                dve.memset(qe[:, b], 0.0).then_inc(zeroed, 1)
            dve.memset(att[:], 0.0).then_inc(zeroed, 1)
            dve.memset(ex[:], 0.0).then_inc(zeroed, 1)
            dve.memset(ones[:], 1.0).then_inc(zeroed, 1)
            dve.wait_ge(st_in, 16)
            dve.wait_ge(filled, 3 + 2 * NL)
            dve.sem_inc(st_set, 1)
            dve.wait_ge(zeroed, 4)

            def exponents(t, b, L):
                dve.wait_ge(g_come[b], came(t, b, 2))
                for l, half in levels(L):
                    bh = halved(bs[:, b, :, 0:L], half)
                    xh = halved(ex[:, b, l, :, 0:L], half)
                    dve.tensor_tensor(xh[:, :, :, 1, :], bh[:, :, :, 1, :],
                                      bh[:, :, :, 0, half - 1:half].to_broadcast([P, 2, L // (2 * half), half]), ALU.subtract)
                dve.tensor_tensor(ex[:, b, E_K, :, 0:L], bs[:, b, :, L - 1:L].to_broadcast([P, 2, L]), bs[:, b, :, 0:L],
                                  ALU.subtract).then_inc(uppers, 1)

            def decayed(t, b, L):
                dve.wait_ge(k_come[b], came(t, b, 3))
                dve.wait_ge(decays, 2 * (t + 2))
                l0 = levels(L)[0][0]
                dve.tensor_tensor(ke[:, b, l0:NL, :, 0:L], kr[:, b:b + 1, :, 0:L].to_broadcast([P, NL - l0, 2, L]),
                                  ex[:, b, l0:NL, :, 0:L], ALU.mult).then_inc(k_ready, 1)
                dve.tensor_tensor(kd[:, b, :, 0:L], kr[:, b, :, 0:L], ex[:, b, E_K, :, 0:L], ALU.mult).then_inc(k_ready, 1)
                n = NL + 1 - l0
                dve.tensor_tensor(qe[0:GK, b, l0:NL + 1, :, 0, 0:L],
                                  qe[0:GK, b, Q_RAW:Q_RAW + 1, :, 0, 0:L].to_broadcast([GK, n, 2, L]),
                                  ex[0:GK, b, l0:NL + 1, :, 0:L], ALU.mult).then_inc(q_ready0, 1)

            def pick(t, b, L):
                dve.wait_ge(p_done, t + 2)
                n = 0 if L == NEW else NL * t + len(levels(NEW))
                for i, (l, half) in enumerate(levels(L)):
                    nb = L // (2 * half)
                    c = (l % 2) * 256
                    if i:
                        dve.wait_ge(level_picked, n + i)
                    dve.memset(tick[:], 0.0)
                    dve.copy_predicated(
                        halved(att[0:L, :, 0:L], half)[:, :, :, 1, :],
                        masks[0:L, l:l + 1, 0:L // 2].rearrange("p o (n h) -> p o n h", h=half).to_broadcast([L, GH, nb, half]).bitcast(U32),
                        ps[0:L, l // 2, c:c + 256].rearrange("p (a t) -> p a t", a=GH)[:, :, 0:L // 2].rearrange("p a (n h) -> p a n h", h=half))\
                        .then_inc(level_picked, 1)
                dve.wait_ge(level_picked, n + len(levels(L)))
                dve.memset(tick[:], 0.0)
                dve.copy_predicated(att[0:L, :, 0:L], ident[0:L, 0:L].unsqueeze(1).to_broadcast([L, GH, L]).bitcast(U32),
                                    ps[0:L, 4, :].rearrange("p (a t) -> p a t", a=GH)[:, :, 0:L]).then_inc(picked, 1)

            def close(t, b, L):
                dve.wait_ge(kv_done, t + 2)
                for h in range(GH):
                    g, e = divmod(h, 2)
                    rows = slice(e * GK, (e + 1) * GK)
                    dve.scalar_tensor_tensor(out=st[rows, g, :], in0=st[rows, g, :], scalar=ex[rows, b, E_B, g, L - 1:L],
                                             in1=ps[rows, 7, g * 256 + e * GV:g * 256 + (e + 1) * GV],
                                             op0=ALU.mult, op1=ALU.add).then_inc(st_new, 1)
                dve.wait_ge(o_out, t + 2)
                dve.wait_ge(g_ready, t + 2)
                dve.wait_ge(o_sq, GH * (t + 2))
                dve.wait_ge(stored[b], stored_before(t, b))
                dve.tensor_tensor(og[0:L, b], ov[0:L, b], sg[0:L, b], ALU.mult).then_inc(gated, 1)

            def between():
                dve.wait_ge(st_stored, 16)
                dve.memset(st[:], 0.0).then_inc(st_set, 1)

            def turn(t, b):
                exponents(t + 1, 1 - b, CH)
                pick(t, b, CH)
                decayed(t + 1, 1 - b, CH)
                close(t, b, CH)

            for step in (exponents, decayed, pick, close):
                step(-1, 1, NEW)
            between()
            exponents(0, 0, CH)
            decayed(0, 0, CH)
            with dve.Fori(0, NCH // 2 - 1) as i:
                turn(2 * i, 0)
                turn(2 * i + 1, 1)
            turn(NCH - 2, 0)
            pick(NCH - 1, 1, CH)
            close(NCH - 1, 1, CH)

def merge(nc, d):
    with ExitStack() as ctx:
        sb, sem, psum = scope(nc, ctx)
        ident = sb("ident_m", [P, P])
        eps = sb("eps_m", [P, 1])
        grow = sb("grow_m", [TT, D])
        wraw = sb("wraw_m", [P, KD, D])
        wsp = sb("wsp_m", [P, 2, KD, D], F32R)
        mix = sb("mix", [TT, 2, D])
        gq = sb("gq", [TT, 2, GH])
        xin = sb("xin_m", [TT, 2, D])
        x2 = sb("x2s", [TT, 2, D])
        xn = sb("xn_m", [TT, 2, D])
        mT = sb("mT", [P, 2, 2, KD, TT], F32R)
        hT = sb("hT_m", [P, 2, KD, TT])
        msq = sb("msq_m", [TT, 2])
        rms = sb("rms_m", [TT, 2])
        inv = sb("inv_m", [TT, 2])
        ps = psum("ps_merge")
        filled, g_in = sem("filled_m"), sem("g_in_m")
        w_come, w_hi, w_lo = [sem(f"wm_come{k}") for k in range(KD)], sem("wm_hi"), sem("wm_lo")
        come, x_come = [sem("mix_come0"), sem("mix_come1")], [sem("xm_come0"), sem("xm_come1")]
        q_root, q_inv, m_ready = sem("q_root"), sem("q_inv"), sem("m_ready")
        m_turned, m_hi, m_lo = sem("m_turned"), sem("m_hi"), sem("m_lo")
        multiplied, added, squared, rooted, inverted, scaled = (
            sem("multiplied"), sem("added"), sem("squared_m"), sem("rooted_m"), sem("inverted_m"), sem("scaled_m"))
        h_turned, h_high, h_low = sem("h_turned"), sem("h_high"), sem("h_low")
        stored = [sem("stored_m0"), sem("stored_m1")]
        block = ctx.enter_context(nc.Block())
        CREDIT = 2

        def steps(e, pre, first, middle, last):
            pre(0, 0)
            pre(1, 1)
            first(0, 0)
            first(1, 1)
            pre(2, 0)
            middle(0, 0)
            with e.Fori(0, NT // 2 - 2) as i:
                first(2 * i + 2, 0)
                pre(2 * i + 3, 1)
                middle(2 * i + 1, 1)
                last(2 * i, 0)
                first(2 * i + 3, 1)
                pre(2 * i + 4, 0)
                middle(2 * i + 2, 0)
                last(2 * i + 1, 1)
            first(NT - 2, 0)
            pre(NT - 1, 1)
            middle(NT - 3, 1)
            last(NT - 4, 0)
            first(NT - 1, 1)
            middle(NT - 2, 0)
            last(NT - 3, 1)
            middle(NT - 1, 1)
            last(NT - 2, 0)
            last(NT - 1, 1)

        @block.sync
        def _(sp):
            for b in range(2):
                sp.sem_inc(stored[b], 32)

            def load_mix(t, b):
                sp.wait_ge(m_turned, t - 1 + CREDIT)
                rows = bass.ds(t * TT, TT)
                sp.dma_start(mix[:, b, 0:FOX], d["mixf"][rows, :]).then_inc(come[b], 16)
                sp.dma_start(mix[:, b, FOX:D], d["mixg"][rows, :]).then_inc(come[b], 16)
                sp.dma_start(gq[:, b], d["gsq"][rows, :]).then_inc(come[b], 16)

            def load_x(t, b, tail=False):
                sp.wait_ge(added, t - 1 + CREDIT)
                if tail:
                    sp.dma_start(xin[0:LAST_PROMPT, b], d["x_prompt"][0, (NT - 1) * TT:SEQ, :]).then_inc(x_come[b], 16)
                    sp.dma_start(xin[LAST_PROMPT:TT, b], d["x_sample"][0]).then_inc(x_come[b], 16)
                else:
                    sp.dma_start(xin[:, b], d["x_prompt"][0, bass.ds(t * TT, TT), :]).then_inc(x_come[b], 16)

            def store(t, b):
                sp.wait_ge(added, t + 1 + CREDIT)
                sp.dma_start(d["x2"][bass.ds(t * TT, TT), :], x2[:, b]).then_inc(stored[b], 16)
                sp.wait_ge(h_low, t + 1 + CREDIT)
                sp.wait_ge(h_high, t + 1 + CREDIT)
                sp.dma_start(d["h2T"][bass.ds(t, 1)].rearrange("o p k t -> (o p) k t"), hT[:, b]).then_inc(stored[b], 16)

            for k in range(KD):
                sp.dma_start(wraw[:, k], d["w_out"][0, k * P:(k + 1) * P, :]).then_inc(w_come[k], 16)
            sp.dma_start(grow[:], d["norm2_g"].partition_broadcast(TT)).then_inc(g_in, 16)
            load_mix(0, 0)
            load_x(0, 0)
            load_mix(1, 1)
            load_x(1, 1)
            load_mix(2, 0)
            load_x(2, 0)
            with sp.Fori(0, NT // 2 - 2) as i:
                load_mix(2 * i + 3, 1)
                load_x(2 * i + 3, 1)
                store(2 * i, 0)
                load_mix(2 * i + 4, 0)
                load_x(2 * i + 4, 0)
                store(2 * i + 1, 1)
            load_mix(NT - 1, 1)
            load_x(NT - 1, 1, tail=True)
            store(NT - 4, 0)
            store(NT - 3, 1)
            store(NT - 2, 0)
            store(NT - 1, 1)
            for b in range(2):
                sp.wait_ge(stored[b], 32 * (NT // 2 + 1))

        @block.gpsimd
        def _(pool):
            pool.memset(eps[:], EPS).then_inc(filled, 1)
            pool.memset(ident[:], 0.0).then_inc(filled, 1)
            pool.wait_ge(filled, 2)
            pool.affine_select(out=ident[:], in_=ident[:], compare_op=ALU.not_equal, fill=1.0, base=0,
                               pattern=[[-1, P]], channel_multiplier=1).then_inc(filled, 1)

        @block.scalar
        def _(act):
            act.sem_inc(h_high, CREDIT)
            act.wait_ge(filled, 3)
            for k in range(KD):
                act.wait_ge(w_come[k], 16)
                act.activation(wsp[:, HI, k], wraw[:, k], ACT.Copy).then_inc(w_hi, 1)

            def pre(t, b):
                act.wait_ge(come[b], 24 * (t - b) + 48)
                act.activation(gq[:, b], gq[:, b], ACT.Sqrt, scale=1.0 / GV, bias=eps[0:TT]).then_inc(q_root, 1)

            def first(t, b):
                act.wait_ge(m_turned, t + 1 + CREDIT)
                act.wait_ge(multiplied, t - 1 + CREDIT)
                act.activation(mT[:, b, HI].rearrange("p (a k) t -> p a (k t)", a=2), ps[:, 0:2, 0:4 * TT], ACT.Copy).then_inc(m_hi, 1)

            def middle(t, b):
                act.wait_ge(added, t + 1 + CREDIT)
                act.activation(xn[:, b], x2[:, b], ACT.Square, accum_out=msq[:, b:b + 1]).then_inc(squared, 1)
                act.wait_ge(squared, t + 1)
                act.activation(rms[:, b:b + 1], msq[:, b:b + 1], ACT.Sqrt, scale=1.0 / D, bias=eps[0:TT]).then_inc(rooted, 1)

            def last(t, b):
                act.wait_ge(h_turned, t + 1)
                act.wait_ge(stored[b], 16 * (t - b) + 32)
                act.activation(hT[:, b, 4:8].rearrange("p k t -> p (k t)"), ps[:, 7, 0:4 * TT], ACT.Copy).then_inc(h_high, 1)

            steps(act, pre, first, middle, last)

        @block.vector
        def _(dve):
            dve.sem_inc(added, CREDIT)
            dve.sem_inc(h_low, CREDIT)
            dve.sem_inc(m_lo, CREDIT)
            dve.wait_ge(g_in, 16)
            for k in range(KD):
                dve.wait_ge(w_hi, k + 1)
                dve.tensor_tensor(wsp[:, LO, k], wraw[:, k], wsp[:, HI, k].bitcast(F32), ALU.subtract).then_inc(w_lo, 1)

            def pre(t, b):
                dve.wait_ge(q_root, t + 1)
                dve.reciprocal(gq[:, b], gq[:, b]).then_inc(q_inv, 1)
                dve.wait_ge(q_inv, t + 1)
                rows = mix[:, b, FOX:D].rearrange("p (h v) -> p h v", h=GH)
                dve.tensor_tensor(rows, rows, gq[:, b].unsqueeze(2).to_broadcast([TT, GH, GV]), ALU.mult).then_inc(m_ready, 1)

            def first(t, b):
                dve.wait_ge(m_hi, t + 1)
                part = lambda s: mT[:, b, s].rearrange("p (a k) t -> p a (k t)", a=2)
                dve.tensor_tensor(part(LO), ps[:, 0:2, 0:4 * TT], part(HI).bitcast(F32), ALU.subtract).then_inc(m_lo, 1)

            def middle(t, b):
                dve.wait_ge(multiplied, t + 1 + CREDIT)
                dve.wait_ge(stored[b], 16 * (t - b) + 32)
                dve.wait_ge(x_come[b], 8 * (t - b) + (32 if isinstance(t, int) and t == NT - 1 else 16))
                dve.tensor_tensor(x2[:, b].rearrange("p (a c) -> p a c", a=2), ps[0:TT, 2 + 2 * b:4 + 2 * b, :],
                                  xin[:, b].rearrange("p (a c) -> p a c", a=2), ALU.add).then_inc(added, 1)
                dve.wait_ge(rooted, t + 1)
                dve.reciprocal(inv[:, b:b + 1], rms[:, b:b + 1]).then_inc(inverted, 1)
                dve.wait_ge(inverted, t + 1)
                dve.scalar_tensor_tensor(out=xn[:, b], in0=x2[:, b], scalar=inv[:, b:b + 1], in1=grow[:],
                                         op0=ALU.mult, op1=ALU.mult).then_inc(scaled, 1)

            def last(t, b):
                dve.wait_ge(h_turned, t + 1)
                dve.wait_ge(stored[b], 16 * (t - b) + 32)
                dve.tensor_copy(hT[:, b, 0:4].rearrange("p k t -> p (k t)"), ps[:, 6, 0:4 * TT]).then_inc(h_low, 1)

            steps(dve, pre, first, middle, last)

        @block.tensor
        def _(pe):
            pe.sem_inc(multiplied, CREDIT)
            pe.sem_inc(m_turned, CREDIT)
            pe.wait_ge(filled, 3)

            def turn(rows, bank0):
                for k in range(KD):
                    last = pe.transpose(ps[:, bank0 + k // 4, (k % 4) * TT:(k % 4 + 1) * TT], rows[:, k * P:(k + 1) * P], ident[0:TT, 0:TT])
                return last

            def first(t, b):
                pe.wait_ge(m_ready, t + 1)
                pe.wait_ge(m_lo, t + CREDIT)
                turn(mix[:, b], 0).then_inc(m_turned, 1)

            def middle(t, b):
                if isinstance(t, int) and t == 0:
                    pe.wait_ge(w_lo, KD)
                pe.wait_ge(m_lo, t + 1 + CREDIT)
                pe.wait_ge(added, t - 1 + CREDIT)
                for n in range(2):
                    m = 0
                    for k in range(KD):
                        for s, v in PASSES:
                            last = pe.matmul(ps[0:TT, 2 + 2 * b + n, :], mT[:, b, s, k, :], wsp[:, v, k, n * 512:(n + 1) * 512],
                                             start=m == 0, stop=m == 3 * KD - 1)
                            m += 1
                last.then_inc(multiplied, 1)

            def last(t, b):
                pe.wait_ge(scaled, t + 1)
                pe.wait_ge(h_low, t + CREDIT)
                pe.wait_ge(h_high, t + CREDIT)
                turn(xn[:, b], 6).then_inc(h_turned, 1)

            steps(pe, lambda t, b: None, first, middle, last)

NF = DFF // P
STEPS = 2 * NF
HT = NT // 2
HTOK = HT * TT
FB = (4, 3, 3)
FB0 = (0, 4, 7, 10)
NFB = len(FB)
YB = 4
DGROUPS = NFB * KD


def ffn(nc, d):
    with ExitStack() as ctx:
        sb, sem, psum = scope(nc, ctx)
        ident = sb("ident_n", [P, P])
        eps = sb("eps_n", [P, 1])
        grow = sb("grow_n", [TT, D])
        hraw = sb("hraw", [P, 2, KD, TT])
        h2 = sb("h2", [P, HT, 2, KD, TT], F32R)
        wraw = sb("wraw_n", [P, 2, KD, P])
        draw = sb("draw", [P, D])
        wsp = sb("wsp_n", [P, 2, 2, 2, KD, P], F32R)
        dsp = sb("dsp", [P, 2, 2, D], F32R)
        silu = sb("silu", [P, 2, FB[0] * TT])
        a32 = sb("a32", [P, 2, FB[0] * TT])
        aT = sb("aT", [P, 2, 2, HTOK], F32R)
        yacc = sb("yacc", [P, KD, HTOK])
        yo = sb("yo", [TT, YB, D])
        msq = sb("msq_n", [TT, 2])
        rms = sb("rms_n", [TT, 2])
        inv = sb("inv_n", [TT, 2])
        ps = psum("ps_ffn")
        filled, g_in, zeroed = sem("filled_n"), sem("g_in_n"), sem("zeroed_n")
        h_come, h_hi, h_lo = [sem("h_come0"), sem("h_come1")], sem("h_hi_n"), sem("h_lo_n")
        gu_come, gu_hi, gu_lo = [sem("gate_come"), sem("up_come")], sem("gu_hi"), sem("gu_lo")
        d_come, d_hi, d_lo = sem("d_come"), sem("d_hi"), sem("d_lo")
        gate_done, up_done = sem("gate_done_n"), sem("up_done")
        exp_done, one_done, inv_done, silu_done = sem("exp_done"), sem("one_done"), sem("inv_done"), sem("silu_done")
        a_made, a_hi, a_lo = sem("a_made"), sem("a_hi"), sem("a_lo")
        down_done, added = sem("down_done"), sem("added_n")
        x_come = [sem(f"x2_come{b}") for b in range(YB)]
        y_turned, y_added, squared, rooted, inverted, y_done = (
            sem("y_turned"), sem("y_added"), sem("squared_n"), sem("rooted_n"), sem("inverted_n"), sem("y_done"))
        y_stored = [sem(f"y_stored{b}") for b in range(YB)]
        block = ctx.enter_context(nc.Block())
        A_CREDIT, ADD_CREDIT = 2, 4

        def cols(b):
            return slice(FB0[b] * TT, FB0[b + 1] * TT)

        def steps(e, prelude, step, between, final):
            prelude()
            step(0, 0, 0, True, False)
            with e.Fori(0, (NF - 2) // 2) as i:
                step(2 * i + 1, 1, 0, True, True)
                step(2 * i + 2, 0, 0, True, True)
            step(NF - 1, 1, 0, True, True, between)
            step(NF, 0, NF, True, True)
            final(0)
            with e.Fori(0, (NF - 2) // 2) as i:
                step(2 * i + NF + 1, 1, NF, True, True)
                step(2 * i + NF + 2, 0, NF, True, True)
            step(STEPS - 1, 1, NF, True, True)
            step(STEPS, 0, NF, False, True)
            final(1)

        def is_last(u):
            return isinstance(u, int) and u >= STEPS - 1

        @block.sync
        def _(sp):
            wg = d["w_gate"][0].rearrange("(k p) f -> p k f", p=P)
            wu = d["w_up"][0].rearrange("(k p) f -> p k f", p=P)

            def load_gu(u, f):
                for s, w in enumerate((wg, wu)):
                    if not isinstance(u, int) or u:
                        sp.wait_ge(gu_lo, 2 * u - 1 + s)
                    sp.dma_start(wraw[:, s], w[:, :, bass.ds(f * P, P)]).then_inc(gu_come[s], 16)

            def load_h(half):
                for t in range(half * HT, (half + 1) * HT):
                    if t >= 2:
                        sp.wait_ge(h_lo, t - 1)
                    sp.dma_start(hraw[:, t % 2], d["h2T"][t]).then_inc(h_come[t % 2], 16)

            def prelude():
                load_gu(0, 0)
                load_h(0)
                sp.dma_start(grow[:], d["final_norm_g"].partition_broadcast(TT)).then_inc(g_in, 16)

            def step(u, par, off, gu, down, between=None):
                if not is_last(u):
                    load_gu(u + 1, 0 if isinstance(u, int) and u == NF - 1 else u + 1 - off)
                if gu:
                    if not isinstance(u, int) or u:
                        sp.wait_ge(d_lo, u)
                    sp.dma_start(draw[:], d["w_down"][0, bass.ds((u - off) * P, P), :]).then_inc(d_come, 16)
                if between:
                    load_h(1)

            def load_x(t):
                if t >= YB:
                    sp.wait_ge(y_stored[t % YB], 16 * (t // YB))
                sp.dma_start(yo[:, t % YB], d["x2"][t * TT:(t + 1) * TT, :]).then_inc(x_come[t % YB], 16)

            def final(half):
                t0 = half * HT
                for t in range(t0, t0 + YB - 1):
                    load_x(t)
                for t in range(t0, t0 + HT):
                    sp.wait_ge(y_done, t + 1)
                    if t < NT - 1:
                        sp.dma_start(d["y_p"][t * TT:(t + 1) * TT, :], yo[:, t % YB]).then_inc(y_stored[t % YB], 16)
                    else:
                        sp.dma_start(d["y_p"][t * TT:SEQ, :], yo[0:LAST_PROMPT, t % YB]).then_inc(y_stored[t % YB], 16)
                        sp.dma_start(d["y_s"][:, :], yo[LAST_PROMPT:TT, t % YB]).then_inc(y_stored[t % YB], 16)
                    if t + YB - 1 < t0 + HT:
                        load_x(t + YB - 1)

            steps(sp, prelude, step, True, final)
            for b in range(YB):
                sp.wait_ge(y_stored[b], 16 * (NT // YB + (b == YB - 1)))

        @block.gpsimd
        def _(pool):
            pool.memset(eps[:], EPS).then_inc(filled, 1)
            pool.memset(ident[:], 0.0).then_inc(filled, 1)
            pool.wait_ge(filled, 2)
            pool.affine_select(out=ident[:], in_=ident[:], compare_op=ALU.not_equal, fill=1.0, base=0,
                               pattern=[[-1, P]], channel_multiplier=1).then_inc(filled, 1)

            def lo_gu(u, par, s):
                pool.wait_ge(gu_hi, 2 * u + s + 1)
                pool.tensor_tensor(wsp[:, par, s, LO], wraw[:, s], wsp[:, par, s, HI].bitcast(F32), ALU.subtract).then_inc(gu_lo, 1)

            def lo_h(half, b):
                for t in range(half * HT + FB0[b], half * HT + FB0[b + 1]):
                    pool.wait_ge(h_hi, t + 1)
                    pool.tensor_tensor(h2[:, t % HT, LO], hraw[:, t % 2], h2[:, t % HT, HI].bitcast(F32), ALU.subtract).then_inc(h_lo, 1)

            def prelude():
                for s in range(2):
                    lo_gu(0, 0, s)
                for b in range(NFB):
                    lo_h(0, b)

            def step(u, par, off, gu, down, between=None):
                if not is_last(u):
                    for s in range(2):
                        lo_gu(u + 1, 1 - par, s)
                        if between and s:
                            lo_h(1, 0)
                if gu:
                    pool.wait_ge(d_hi, u + 1)
                    pool.tensor_tensor(dsp[:, par, LO], draw[:], dsp[:, par, HI].bitcast(F32), ALU.subtract).then_inc(d_lo, 1)
                if between:
                    for b in range(1, NFB):
                        lo_h(1, b)

            def final(half):
                if not half:
                    for t in range(HT):
                        pool.wait_ge(y_turned, t + 1)
                        pool.memset(yacc[:, :, t * TT:(t + 1) * TT], 0.0).then_inc(zeroed, 1)

            steps(pool, prelude, step, True, final)

        @block.scalar
        def _(act):
            act.wait_ge(filled, 3)

            def hi_gu(u, par, s):
                act.wait_ge(gu_come[s], 16 * (u + 1))
                act.activation(wsp[:, par, s, HI], wraw[:, s], ACT.Copy).then_inc(gu_hi, 1)

            def hi_h(half, b):
                if half:
                    act.wait_ge(up_done, NFB * (NF - 1) + b + 1)
                for t in range(half * HT + FB0[b], half * HT + FB0[b + 1]):
                    act.wait_ge(h_come[t % 2], 16 * (t // 2 + 1))
                    act.activation(h2[:, t % HT, HI], hraw[:, t % 2], ACT.Copy).then_inc(h_hi, 1)

            def prelude():
                for s in range(2):
                    hi_gu(0, 0, s)
                for b in range(NFB):
                    hi_h(0, b)

            def step(u, par, off, gu, down, between=None):
                for b in range(NFB):
                    if gu:
                        act.wait_ge(gate_done, NFB * u + b + 1)
                        act.activation(silu[:, (par + b) % 2, 0:FB[b] * TT], ps[:, 2 * ((par + b) % 2), 0:FB[b] * TT], ACT.Exp,
                                       scale=-1.0).then_inc(exp_done, 1)
                    if b < 2 and not is_last(u):
                        hi_gu(u + 1, 1 - par, b)
                    if b == 2 and gu:
                        act.wait_ge(d_come, 16 * (u + 1))
                        act.activation(dsp[:, par, HI], draw[:], ACT.Copy).then_inc(d_hi, 1)
                    if gu:
                        act.wait_ge(a_made, NFB * u + b + 1 + A_CREDIT)
                        act.activation(aT[:, par, HI, cols(b)], a32[:, (par + b) % 2, 0:FB[b] * TT], ACT.Copy).then_inc(a_hi, 1)
                    if between and b:
                        hi_h(1, b - 1)
                if between:
                    hi_h(1, NFB - 1)

            def final(half):
                for t in range(half * HT, (half + 1) * HT):
                    b = t % 2
                    act.wait_ge(y_added, t + 1)
                    act.activation(ps[0:TT, 4 + 2 * b:6 + 2 * b, :].rearrange("p a c -> p (a c)"), yo[:, t % YB], ACT.Square,
                                   accum_out=msq[:, b:b + 1]).then_inc(squared, 1)
                    act.wait_ge(squared, t + 1)
                    act.activation(rms[:, b:b + 1], msq[:, b:b + 1], ACT.Sqrt, scale=1.0 / D, bias=eps[0:TT]).then_inc(rooted, 1)

            steps(act, prelude, step, True, final)

        @block.vector
        def _(dve):
            dve.sem_inc(a_made, A_CREDIT)
            dve.sem_inc(added, ADD_CREDIT)
            dve.memset(yacc[:], 0.0).then_inc(zeroed, 1)
            dve.wait_ge(zeroed, 1)
            dve.wait_ge(g_in, 16)

            def adds(v, slot):
                b = slot // 2
                for i in range(4):
                    n = DGROUPS * v + 4 * slot + i
                    y = yacc[:, 4 * (slot % 2) + i, cols(b)]
                    dve.wait_ge(down_done, n + 1)
                    dve.tensor_tensor(y, ps[:, 4 + i, 0:FB[b] * TT], y, ALU.add).then_inc(added, 1)

            def step(u, par, off, gu, down, between=None):
                for b in range(NFB):
                    w = FB[b] * TT
                    q = (par + b) % 2
                    x = silu[:, q, 0:w]
                    n = NFB * u + b + 1
                    if down:
                        adds(u - 1, 2 * b)
                    if gu:
                        dve.wait_ge(exp_done, n)
                        dve.tensor_scalar(x, x, 1.0, None, ALU.add).then_inc(one_done, 1)
                        dve.wait_ge(one_done, n)
                        dve.reciprocal(x, x).then_inc(inv_done, 1)
                        dve.wait_ge(inv_done, n)
                        dve.tensor_tensor(x, ps[:, 2 * q, 0:w], x, ALU.mult).then_inc(silu_done, 1)
                    if down:
                        adds(u - 1, 2 * b + 1)
                    if gu:
                        dve.wait_ge(silu_done, n)
                        dve.wait_ge(up_done, n)
                        dve.tensor_tensor(a32[:, q, 0:w], ps[:, 2 * q + 1, 0:w], x, ALU.mult).then_inc(a_made, 1)
                        dve.wait_ge(a_hi, n)
                        dve.tensor_tensor(aT[:, par, LO, cols(b)], a32[:, q, 0:w], aT[:, par, HI, cols(b)].bitcast(F32),
                                          ALU.subtract).then_inc(a_lo, 1)

            def add_x(t):
                b = t % 2
                dve.wait_ge(y_turned, t + 1)
                dve.wait_ge(x_come[t % YB], 16 * (t // YB + 1))
                rows = yo[:, t % YB].rearrange("p (a c) -> p a c", a=2)
                dve.tensor_tensor(rows, ps[0:TT, 2 * b:2 * b + 2, :], rows, ALU.add).then_inc(y_added, 1)

            def final(half):
                add_x(half * HT)
                for t in range(half * HT, (half + 1) * HT):
                    b = t % 2
                    if t + 1 < (half + 1) * HT:
                        add_x(t + 1)
                    dve.wait_ge(rooted, t + 1)
                    dve.reciprocal(inv[:, b:b + 1], rms[:, b:b + 1]).then_inc(inverted, 1)
                    dve.wait_ge(inverted, t + 1)
                    dve.scalar_tensor_tensor(out=yo[:, t % YB], in0=yo[:, t % YB], scalar=inv[:, b:b + 1], in1=grow[:],
                                             op0=ALU.mult, op1=ALU.mult).then_inc(y_done, 1)
                if not half:
                    dve.wait_ge(zeroed, 1 + HT)

            steps(dve, lambda: None, step, True, final)

        @block.tensor
        def _(pe):
            pe.wait_ge(filled, 3)

            def gate_up(u, par, b, s, start):
                q = (par + b) % 2
                if b == 0:
                    pe.wait_ge(gu_lo, 2 * u + s + 1)
                if s == 0:
                    pe.wait_ge(a_made, NFB * u + b - 1 + A_CREDIT)
                    if start is not None:
                        pe.wait_ge(h_lo, start * HT + FB0[b + 1])
                m = 0
                for k in range(KD):
                    for w, v in PASSES:
                        last = pe.matmul(ps[:, 2 * q + s, 0:FB[b] * TT], wsp[:, par, s, w, k, :], h2[:, FB0[b]:FB0[b + 1], v, k, :],
                                         start=m == 0, stop=m == 3 * KD - 1)
                        m += 1
                last.then_inc((gate_done, up_done)[s], 1)

            def downs(v, par, slot):
                b = slot // 2
                if slot % 2 == 0:
                    pe.wait_ge(a_lo, NFB * v + b + 1)
                if slot == 0:
                    pe.wait_ge(d_lo, v + 1)
                for i in range(4):
                    c = (4 * (slot % 2) + i) * P
                    pe.wait_ge(added, DGROUPS * v + 4 * slot + i - 3 + ADD_CREDIT)
                    for m, (w, x) in enumerate(PASSES):
                        last = pe.matmul(ps[:, 4 + i, 0:FB[b] * TT], dsp[:, par, w, c:c + P], aT[:, par, x, cols(b)],
                                         start=m == 0, stop=m == 2)
                    last.then_inc(down_done, 1)

            def step(u, par, off, gu, down, between=None):
                start = u // NF if isinstance(u, int) and u in (0, NF) else None
                for slot in range(2 * NFB):
                    if gu:
                        gate_up(u, par, slot // 2, slot % 2, start)
                    if down:
                        downs(u - 1, 1 - par, slot)

            def final(half):
                pe.wait_ge(added, DGROUPS * NF * (half + 1) + ADD_CREDIT)
                if half == 0:
                    pe.wait_ge(a_made, NFB * (NF + 1) + A_CREDIT)
                for t in range(half * HT, (half + 1) * HT):
                    if t >= half * HT + 2:
                        pe.wait_ge(y_added, t - 1)
                    for c in range(KD):
                        last = pe.transpose(ps[0:TT, 2 * (t % 2) + c // 4, (c % 4) * P:(c % 4 + 1) * P],
                                            yacc[:, c, (t % HT) * TT:(t % HT + 1) * TT], ident[:])
                    last.then_inc(y_turned, 1)
                if half == 0:
                    pe.wait_ge(y_added, HT)
                    pe.wait_ge(squared, HT)

            steps(pe, lambda: None, step, True, final)


SCRATCH = {
    "kbias": ((HEADS, NTOK), F32), "pbias": ((HEADS, PAST), F32), "gsum": ((GKW, NTOK), F32),
    "mixf": ((NTOK, FOX), F32), "mixg": ((NTOK, GVW), F32), "gsq": ((NTOK, GH), F32),
    "x2": ((NTOK, D), F32), "h2T": ((NT, P, KD, TT), F32),
    "zT": ((R_GG + RANK, NTOK), F32), "zrow": ((NTOK, 2 * GVW), F32),
}
OUTPUTS = {
    "y_p": ((SEQ, D), F32), "y_s": ((NEW, D), F32),
    "new_k_p": ((SEQ, FOX), F32), "new_v_p": ((SEQ, FOX), F32), "new_f_p": ((SEQ, HEADS), F32),
    "st_p": ((GH * GK, GV), F32),
    "new_k_s": ((NEW, FOX), F32), "new_v_s": ((NEW, FOX), F32), "new_f_s": ((NEW, HEADS), F32),
    "st_s": ((GH * GK, GV), F32),
}


def stream_step(nc, d):
    for name, (shape, dt) in SCRATCH.items():
        d[name] = nc.dram_tensor(name, shape, dt, kind="Internal").ap()
    project(nc, d)
    gates(nc, d)
    fox_prompt(nc, d)
    fox_sample(nc, d)
    gla(nc, d)
    merge(nc, d)
    ffn(nc, d)


_INS = ['x_prompt', 'x_sample', 'cache_fox_k', 'cache_fox_v', 'cache_fox_logf', 'state_gla', 'norm1_g', 'w_in', 'w_gate2',
        'b_gate2', 'b_forget', 'gla_norm_g', 'w_out', 'norm2_g', 'w_gate', 'w_up', 'w_down', 'final_norm_g']
_SHAPES = [(1, SEQ, D), (1, NEW, D),
           (1, 1, SEQ, HEADS, HD), (1, 1, SEQ, HEADS, HD), (1, 1, SEQ, HEADS), (1, 1, GH, GK, GV),
           (1, 1, NEW, HEADS, HD), (1, 1, NEW, HEADS, HD), (1, 1, NEW, HEADS), (1, 1, GH, GK, GV)]


def kernel(**inputs):
    import concourse.bacc as _bacc
    from concourse.bass_utils import run_bass_kernel_spmd as _run

    nc = _bacc.Bacc("TRN2", target_bir_lowering=False, num_devices=1)
    arrays, d = {}, {}
    for name in _INS:
        a = np.ascontiguousarray(inputs[name])
        arrays[f"in_{name}_dram"] = a
        d[name] = nc.dram_tensor(f"in_{name}_dram", a.shape, mybir.dt.from_np(a.dtype), kind="ExternalInput").ap()
    for name, (shape, dt) in OUTPUTS.items():
        d[name] = nc.dram_tensor(f"out_{name}_dram", shape, dt, kind="ExternalOutput").ap()
    stream_step(nc, d)
    r = _run(nc, [arrays], core_ids=[0])
    return tuple(r.results[0][f"out_{name}_dram"].reshape(shape) for name, shape in zip(OUTPUTS, _SHAPES))
```
